# Optimizing a Trainium2 kernel written in Bass

```python
import math
import jax, jax.numpy as jnp
from jax import lax
import numpy as np

D_MODEL = 2048
BATCH = 1
SEQ = 256
DEPTH = 1

CHUNK = 64
Q_BLOCK = 128
MIX_WIDTH = D_MODEL
ATTN_WIDTH = MIX_WIDTH // 2
RET_WIDTH = MIX_WIDTH - ATTN_WIDTH
ATTN_HEADS = 8
HEAD_DIM = ATTN_WIDTH // ATTN_HEADS
KV_HEADS = 2
KV_WIDTH = KV_HEADS * HEAD_DIM
IDX_HEADS = 16
IDX_DIM = 64
TOPK_MAX = 256
RET_HEADS = 8
RET_DK = RET_WIDTH // RET_HEADS
RET_DV = RET_WIDTH // RET_HEADS
ROT_BASE = 10000.0
N_GROUPS = 4
EXPERTS_PER_GROUP = 8
N_EXPERTS = N_GROUPS * EXPERTS_PER_GROUP
TOP_EXPERTS = 2
EXPERT_FF = D_MODEL // 4
EPS = 1e-6

IN_SPLITS = (ATTN_WIDTH, KV_WIDTH, KV_WIDTH,
             IDX_HEADS * IDX_DIM, IDX_DIM, IDX_HEADS,
             RET_WIDTH, RET_WIDTH, RET_WIDTH, RET_WIDTH)
IN_WIDTH = sum(IN_SPLITS)

kernel_name = "hybrid_dsa_retention_hmoe"

def rms_norm(x, g):
    xf = x.astype(jnp.float32)
    y = xf * lax.rsqrt(jnp.mean(xf * xf, axis=-1, keepdims=True) + EPS)
    return (y * g.astype(jnp.float32)).astype(x.dtype)

def layer_norm(x, w, b):
    xf = x.astype(jnp.float32)
    mu = jnp.mean(xf, axis=-1, keepdims=True)
    var = jnp.mean(jnp.square(xf - mu), axis=-1, keepdims=True)
    y = (xf - mu) * lax.rsqrt(var + EPS)
    return (y * w.astype(jnp.float32) + b.astype(jnp.float32)).astype(x.dtype)

def split_columns(a, sizes):
    out, start = [], 0
    for s in sizes:
        out.append(a[..., start:start + s])
        start += s
    return out

def rotate(x, pos):
    half = x.shape[-1] // 2
    inv = 1.0 / (ROT_BASE ** jnp.linspace(0.0, 1.0, half, dtype=jnp.float32))
    ang = pos[:, None] * inv[None, :]
    c = jnp.cos(ang)[None, :, None, :]
    s = jnp.sin(ang)[None, :, None, :]
    x1, x2 = x[..., :half], x[..., half:]
    return jnp.concatenate([x1 * c - x2 * s, x1 * s + x2 * c], axis=-1)

def dsa_attention(q, k, v, qi, ki, wi):
    B, S = q.shape[0], q.shape[1]
    topk = min(TOPK_MAX, S // 4)
    nb = S // Q_BLOCK
    key_chunk = jnp.arange(S) // CHUNK
    ki32 = ki.astype(jnp.float32)

    def to_blocks(a):
        return a.reshape((B, nb, Q_BLOCK) + a.shape[2:]).swapaxes(0, 1)

    def block(args):
        qb, qib, wib, start = args
        q_chunk = (start + jnp.arange(Q_BLOCK)) // CHUNK
        visible = key_chunk[None, :] <= q_chunk[:, None]
        dots = jnp.einsum('bthd,bsd->bths', qib.astype(jnp.float32), ki32)
        score = jnp.einsum('bths,bth->bts', jax.nn.relu(dots), wib.astype(jnp.float32))
        score = jnp.where(visible[None], score, -jnp.inf)
        _, idx = lax.top_k(score, topk)
        valid = key_chunk[idx] <= q_chunk[None, :, None]
        ks = jax.vmap(lambda kb, ib: kb[ib])(k, idx)
        vs = jax.vmap(lambda vb, ib: vb[ib])(v, idx)
        qg = qb.reshape(B, Q_BLOCK, KV_HEADS, ATTN_HEADS // KV_HEADS, HEAD_DIM)
        s = jnp.einsum('btgrd,btkgd->btgrk', qg, ks).astype(jnp.float32) * (HEAD_DIM ** -0.5)
        s = jnp.where(valid[:, :, None, None, :], s, -jnp.inf)
        p = jax.nn.softmax(s, axis=-1).astype(v.dtype)
        o = jnp.einsum('btgrk,btkgd->btgrd', p, vs)
        return o.reshape(B, Q_BLOCK, ATTN_WIDTH)

    starts = jnp.arange(nb) * Q_BLOCK
    out = lax.map(block, (to_blocks(q), to_blocks(qi), to_blocks(wi), starts))
    return out.swapaxes(0, 1).reshape(B, S, ATTN_WIDTH)

def retention(q, k, v):
    B, S, H, dk = q.shape
    dv = v.shape[-1]
    nc = S // CHUNK
    log_gamma = jnp.log1p(-jnp.exp2(-5.0 - jnp.arange(H, dtype=jnp.float32)))
    n = jnp.arange(CHUNK, dtype=jnp.float32)
    rel = n[:, None] - n[None, :]
    intra = jnp.where(rel >= 0, jnp.exp(log_gamma[:, None, None] * jnp.maximum(rel, 0.0)), 0.0)
    cross_decay = jnp.exp(log_gamma[:, None] * (n + 1.0))[..., None]
    state_decay = jnp.exp(log_gamma[:, None] * (CHUNK - 1.0 - n))[..., None]
    chunk_decay = jnp.exp(log_gamma * CHUNK)[:, None, None]

    def to_chunks(a):
        return a.reshape(B, nc, CHUNK, H, a.shape[-1]).transpose(1, 0, 3, 2, 4)

    def step(R, inp):
        qc, kc, vc = inp
        inner = jnp.einsum('bhnd,bhmd->bhnm', qc, kc) * intra
        o = jnp.einsum('bhnm,bhme->bhne', inner, vc) + jnp.einsum('bhnd,bhde->bhne', qc, R) * cross_decay
        R = R * chunk_decay + jnp.einsum('bhmd,bhme->bhde', kc * state_decay, vc)
        return R, o

    R0 = jnp.zeros((B, H, dk, dv), jnp.float32)
    _, o = lax.scan(step, R0, (to_chunks(q), to_chunks(k), to_chunks(v)))
    return o.transpose(1, 0, 3, 2, 4).reshape(B, S, H, dv)

def hier_moe(h, w_group, w_router, w1, w3, w2):
    B, S, D = h.shape
    hf = h.reshape(B * S, D)
    h32 = hf.astype(jnp.float32)
    g_logits = h32 @ w_group.astype(jnp.float32)
    g_prob = jax.nn.softmax(g_logits, axis=-1)
    g_sel = jnp.argmax(g_logits, axis=-1)
    g_gate = jnp.take_along_axis(g_prob, g_sel[:, None], axis=-1)
    e_logits = jnp.einsum('nd,gde->nge', h32, w_router.astype(jnp.float32))
    e_logits = jnp.take_along_axis(e_logits, g_sel[:, None, None], axis=1)[:, 0]
    top_v, top_i = lax.top_k(e_logits, TOP_EXPERTS)
    top_w = jax.nn.softmax(top_v, axis=-1) * g_gate
    expert_id = g_sel[:, None] * EXPERTS_PER_GROUP + top_i
    comb = jnp.sum(jax.nn.one_hot(expert_id, N_EXPERTS, dtype=jnp.float32) * top_w[..., None], axis=1)
    a = jnp.einsum('nd,edf->nef', hf, w1)
    b = jnp.einsum('nd,edf->nef', hf, w3)
    y = jnp.einsum('nef,efd->nd', jax.nn.silu(a) * b * comb[..., None].astype(h.dtype), w2)
    return y.reshape(B, S, D)

def setup_inputs(seed: int = 0) -> dict:
    key = jax.random.key(seed)
    ks = jax.random.split(key, 16)
    f32 = jnp.float32

    def nrm(k, shape, fan_in):
        return jax.random.normal(k, shape, f32) * (fan_in ** -0.5)

    def gain(k, shape):
        return 1.0 + 0.01 * jax.random.normal(k, shape, f32)

    return {
        "x": jax.random.normal(ks[0], (BATCH, SEQ, D_MODEL), f32),
        "norm1_g": gain(ks[1], (DEPTH, D_MODEL)),
        "w_in": nrm(ks[2], (DEPTH, D_MODEL, IN_WIDTH), D_MODEL),
        "q_norm_g": gain(ks[3], (DEPTH, HEAD_DIM)),
        "k_norm_g": gain(ks[4], (DEPTH, HEAD_DIM)),
        "idx_k_ln_w": gain(ks[5], (DEPTH, IDX_DIM)),
        "idx_k_ln_b": 0.01 * jax.random.normal(ks[6], (DEPTH, IDX_DIM), f32),
        "ret_norm_g": gain(ks[7], (DEPTH, RET_WIDTH)),
        "w_out": nrm(ks[8], (DEPTH, MIX_WIDTH, D_MODEL), MIX_WIDTH),
        "norm2_g": gain(ks[9], (DEPTH, D_MODEL)),
        "w_group": nrm(ks[10], (DEPTH, D_MODEL, N_GROUPS), D_MODEL),
        "w_router": nrm(ks[11], (DEPTH, N_GROUPS, D_MODEL, EXPERTS_PER_GROUP), D_MODEL),
        "w1": nrm(ks[12], (DEPTH, N_EXPERTS, D_MODEL, EXPERT_FF), D_MODEL),
        "w3": nrm(ks[13], (DEPTH, N_EXPERTS, D_MODEL, EXPERT_FF), D_MODEL),
        "w2": nrm(ks[14], (DEPTH, N_EXPERTS, EXPERT_FF, D_MODEL), EXPERT_FF),
    }

def reference(x, norm1_g, w_in, q_norm_g, k_norm_g, idx_k_ln_w, idx_k_ln_b, ret_norm_g,
              w_out, norm2_g, w_group, w_router, w1, w3, w2):
    B, S, _ = x.shape
    pos = jnp.arange(S, dtype=jnp.float32)
    idx_w_scale = (IDX_HEADS ** -0.5) * (IDX_DIM ** -0.5)
    for l in range(DEPTH):
        h = rms_norm(x, norm1_g[l])
        proj = h @ w_in[l]
        aq, ak, av, iq, ik, iw, rq, rk, rv, rg = split_columns(proj, IN_SPLITS)

        aq = rms_norm(aq.reshape(B, S, ATTN_HEADS, HEAD_DIM), q_norm_g[l])
        ak = rms_norm(ak.reshape(B, S, KV_HEADS, HEAD_DIM), k_norm_g[l])
        av = av.reshape(B, S, KV_HEADS, HEAD_DIM)
        iq = iq.reshape(B, S, IDX_HEADS, IDX_DIM)
        ik = layer_norm(ik, idx_k_ln_w[l], idx_k_ln_b[l])
        iw = iw * idx_w_scale
        attn_out = dsa_attention(aq, ak, av, iq, ik, iw)

        rq = rotate(rq.reshape(B, S, RET_HEADS, RET_DK).astype(jnp.float32), pos)
        rk = rotate(rk.reshape(B, S, RET_HEADS, RET_DK).astype(jnp.float32), pos) * (RET_DK ** -0.5)
        rv = rv.reshape(B, S, RET_HEADS, RET_DV).astype(jnp.float32)
        ret = retention(rq, rk, rv)
        ret = rms_norm(ret, ret_norm_g[l].reshape(RET_HEADS, RET_DV)).reshape(B, S, RET_WIDTH)
        ret_out = (jax.nn.silu(rg.astype(jnp.float32)) * ret).astype(x.dtype)

        mixed = jnp.concatenate([attn_out.astype(x.dtype), ret_out], axis=-1) @ w_out[l]
        x = x + mixed

        x = x + hier_moe(rms_norm(x, norm2_g[l]), w_group[l], w_router[l], w1[l], w3[l], w2[l])
    return x


_drawn_inputs = setup_inputs


def setup_inputs(seed=0):
    import zlib

    import numpy as np

    out = dict(_drawn_inputs(seed))
    spreads = {}
    factors = {'q_norm_g': 5.297,
     'k_norm_g': 6.074,
     'idx_k_ln_b': 4.309,
     'ret_norm_g': 4.447,
     'norm2_g': 3.047}
    for name, (base, spread) in spreads.items():
        noise = np.random.default_rng([zlib.crc32(name.encode()), seed]).standard_normal(out[name].shape)
        drawn = base * np.exp(spread * noise) if base else spread * noise
        out[name] = __import__('jax').numpy.asarray(drawn.astype(out[name].dtype))
    for name, factor in factors.items():
        out[name] = (out[name] * factor).astype(out[name].dtype)
    return out
```

```python
import math
from contextlib import ExitStack

import numpy as np

import concourse.bass as bass
from concourse import mybir

F32 = mybir.dt.float32
I32 = mybir.dt.int32
U32 = mybir.dt.uint32
ALU = mybir.AluOpType
ACT = mybir.ActivationFunctionType
AX = mybir.AxisListType.X

P = 128
SEQ, D = 256, 2048
TH = SEQ // P
C = D // P
CHUNK = 64
HEADS, HD, KV = 8, 128, 2
IH, ID = 16, 64
TOPK = min(256, SEQ // 4)
GROUPS, PER_GROUP = 4, 8
EXPERTS, FF = 32, 512
J = FF // P
EPS = 1e-6
IN_WIDTH = 1024 + 256 + 256 + 1024 + 64 + 16 + 4 * 1024
AQ, AK, AV, IQ, IK, IW, RQ, RK, RV, RG = 0, 1024, 1280, 1536, 2560, 2624, 2640, 3664, 4688, 5712
NB = 512
FULL = IN_WIDTH // NB
TAIL = IN_WIDTH - FULL * NB
SLOTS = 64
PAIRS = EXPERTS // 2
PASSES = SEQ // SLOTS
SENT, HIDDEN, OFF = -3.0e38, -1.0e38, -1.0e30

RING = 12
BLOCK_CHUNKS = 4
TAIL_CHUNK = FULL * BLOCK_CHUNKS
OUT_CHUNK = TAIL_CHUNK + 1
MOE_CHUNK = OUT_CHUNK + C
PAIR_CHUNKS = 24

IDENT, BEFORE, ONES, COS, SIN, REL, IOTA = 0, 128, 256, 384, 512, 640, 896
CONSTS = IOTA + SEQ
SSQ, RSTD, QKS, QKR, MU, VAR, M8, NEG, SUM, RCP, RETS, RETR, FLAG = 0, 2, 4, 24, 44, 48, 52, 68, 84, 100, 116, 132, 148
LOG_GAMMA = [math.log1p(-2.0 ** (-5 - h)) for h in range(HEADS)]


def chunk_slot(k):
    return k % RING


def chunk_landed(k):
    return 16 * (k // RING + 1)


def build(nc, x, norm1_g, w_in, q_norm_g, k_norm_g, idx_k_ln_w, idx_k_ln_b, ret_norm_g, w_out,
          norm2_g, w_group, w_router, w1, w3, w2, consts, out):
    ctx = ExitStack()
    with ctx:
        def sb(name, shape, dt=F32):
            return ctx.enter_context(nc.sbuf_tensor(name, shape, dt))

        def sem(name):
            return ctx.enter_context(nc.semaphore(name))

        ring = sb("ring", [P, RING, 2048])
        xs = sb("xs", [P, TH, D])
        flat = sb("flat", [P, TH * IN_WIDTH])
        buf_a = sb("buf_a", [P, 4096])
        buf_b = sb("buf_b", [P, 4096])
        const = sb("const", [P, CONSTS])
        st = sb("st", [P, 160])
        flag = sb("flag", [P, 1], I32)
        idx8 = sb("idx8", [P, TH, 2, 8], U32)
        p_t = sb("p_t", [P, 2, 512])
        ps = ctx.enter_context(nc.psum_tensor("ps", [P, 8, 512], F32))

        proj = flat[:, :].rearrange("p (t n) -> p t n", t=TH)
        ident = const[:, IDENT:IDENT + P]
        before = const[:, BEFORE:BEFORE + P]
        ones = const[:, ONES:ONES + P]
        iota = const[:, IOTA:IOTA + SEQ]

        h = buf_a[:, :].rearrange("p (t n) -> p t n", t=TH)
        hT = buf_b[:, :].rearrange("p (c t) -> p c t", c=C)
        g_row = flat[:, 0:D]
        g2_row = flat[:, RV:RV + D]
        sq = buf_a[:, 2048:2048 + 1280]
        gain_q = buf_a[:, 3328:3456]
        gain_k = buf_a[:, 3456:3584]
        ln_w = buf_a[:, 3584:3648]
        ln_b = buf_a[:, 3648:3712]
        ik_dup = buf_a[:, 3712:3968].rearrange("p (t n) -> p t n", t=TH)
        exp_g = buf_b[:, 0:2048].rearrange("p (t n) -> p t n", t=TH)
        aqT = buf_b[:, 0:2048].rearrange("p (h t) -> p h t", h=HEADS)
        iqT = buf_b[:, 2048:4096].rearrange("p (h t) -> p h t", h=IH // 2)
        rkT, rqT = aqT, iqT
        akT = buf_a[:, 0:512].rearrange("p (h t) -> p h t", h=KV)
        ikT = buf_a[:, 512:768]
        score = buf_a[:, 768:1280].rearrange("p (t s) -> p t s", t=TH)
        bias = buf_a[:, 1280:1792].rearrange("p (t s) -> p t s", t=TH)
        relu = buf_a[:, 1792:2816].rearrange("p (b n) -> p b n", b=2)
        prob = buf_a[:, 2816:3840].rearrange("p (b h s) -> p b h s", b=2, h=2)
        decay = buf_a[:, 1792:2304].rearrange("p (b n) -> p b n", b=2)
        inner = buf_a[:, 512:1280].rearrange("p (b n) -> p b n", b=2)
        gain_r = buf_a[:, 2816:3840]
        sq_r = buf_b[:, 2048:4096].rearrange("p (t n) -> p t n", t=TH)

        def mixedT(c, n=1):
            base = (IN_WIDTH if c % 8 >= 4 else 0) + (IQ if c >= HEADS else 0) + (c % 4) * SEQ
            return flat[:, base:base + n * SEQ]

        rb = IN_WIDTH + RV
        gates_w = flat[:, rb:rb + C * 36].rearrange("p (c n) -> p c n", c=C)
        stage_g = flat[:, rb + 576:rb + 640].rearrange("p (c n) -> p c n", c=C)
        stage_r = flat[:, rb + 640:rb + 1152].rearrange("p (g c n) -> p g c n", g=GROUPS, c=C)
        logit = flat[:, rb + 1152:rb + 1224].rearrange("p (t n) -> p t n", t=TH)
        g_pad = flat[:, rb + 1224:rb + 1240].rearrange("p (t n) -> p t n", t=TH)
        g_exp = flat[:, rb + 1240:rb + 1248].rearrange("p (t n) -> p t n", t=TH)
        pick = flat[:, rb + 1248:rb + 1312].rearrange("p (t g n) -> p t g n", t=TH, g=GROUPS)
        e_sel = flat[:, rb + 1312:rb + 1328].rearrange("p (t n) -> p t n", t=TH)
        top8 = flat[:, rb + 1328:rb + 1360].rearrange("p (t a n) -> p t a n", t=TH, a=2)
        idxf = flat[:, rb + 1360:rb + 1392].rearrange("p (t a n) -> p t a n", t=TH, a=2)
        oh = flat[:, rb + 1392:rb + 1440].rearrange("p (t a n) -> p t a n", t=TH, a=3)
        cs = flat[:, rb + 1440:rb + 1472].rearrange("p (t a n) -> p t a n", t=TH, a=2)
        small = flat[:, rb + 1472:rb + 1488].rearrange("p (t n) -> p t n", t=TH)
        comb = flat[:, rb + 1488:rb + 1552].rearrange("p (t e) -> p t e", t=TH)
        sel = flat[:, rb + 1552:rb + 1616].rearrange("p (t e) -> p t e", t=TH)
        posm = flat[:, rb + 1616:rb + 1680].rearrange("p (t e) -> p t e", t=TH)

        h_e = flat[:, 0:2048].rearrange("p (c s) -> p c s", c=C)
        y_sb = flat[:, 2048:4096]
        pick_p = flat[:, 6800:7056].rearrange("p (t e s) -> p t e s", t=TH, e=2)
        gate_p = flat[:, 7056:7312].rearrange("p (t e s) -> p t e s", t=TH, e=2)
        gate_T = flat[:, 7312:7568]
        e_sb = flat[:, 7568:8080]
        hm = flat[:, 8080:8592]
        hm_T = flat[:, 8592:9104].rearrange("p (j s) -> p j s", j=J)

        x_v = x.rearrange("b (t p) d -> (b t) p d", p=P)
        out_v = out.rearrange("b (t p) d -> (b t) p d", p=P)
        w_in_v = w_in.rearrange("l (p c) n -> (l p) c n", c=C)
        w_out_v = w_out.rearrange("l (c p) n -> (l c) p n", p=P)
        w1_v = w1.rearrange("l e (p c) f -> (l e) p (c f)", c=C)
        w3_v = w3.rearrange("l e (p c) f -> (l e) p (c f)", c=C)
        w2_v = w2.rearrange("l e (p j) n -> (l e) p (j n)", j=J)

        landed = [sem(f"landed{i}") for i in range(RING)]
        x_in = [sem("x_in0"), sem("x_in1")]
        const_in, g1_in, gains_in = sem("const_in"), sem("g1_in"), sem("gains_in")
        ret_gain_in, g2_in, router_in = sem("ret_gain_in"), sem("g2_in"), sem("router_in")
        stored = sem("stored")
        ring_used = sem("ring_used")
        ssq_done, root_done = sem("ssq_done"), sem("root_done")
        h_done, hT_full = sem("h_done"), sem("hT_full")
        bank_free = sem("bank_free")
        hT_by_dve = sem("hT_by_dve")
        block_done = sem("block_done")
        qk_ssq, qk_root, qk_done = sem("qk_ssq"), sem("qk_root"), sem("qk_done")
        eps_set = sem("eps_set")
        index_ready, rotated, silu_exp, silu_done = sem("index_ready"), sem("rotated"), sem("silu_exp"), sem("silu_done")
        bank_full, act_freed, dve_freed = sem("bank_full"), sem("act_freed"), sem("dve_freed")
        relu_read = sem("relu_read")
        scored, exp_done, prob_ready = sem("scored"), sem("exp_done"), sem("prob_ready")
        decay_ready, inner_ready = sem("decay_ready"), sem("inner_ready")
        ret_ssq, ret_root, ret_ready = sem("ret_ssq"), sem("ret_root"), sem("ret_ready")
        mixed_done, x2_done = sem("mixed_done"), sem("x2_done")
        logits_done, logits_read = sem("logits_done"), sem("logits_read")
        g_max, g_expd, e_max, e_expd = sem("g_max"), sem("g_expd"), sem("e_max"), sem("e_expd")
        sel_ready, ranks_done, flag_ready = sem("sel_ready"), sem("ranks_done"), sem("flag_ready")
        pick_ready, gather_done, h_e_ready = sem("pick_ready"), sem("gather_done"), sem("h_e_ready")
        gate_ready, gate_turned, gate_T_ready = sem("gate_ready"), sem("gate_turned"), sem("gate_T_ready")
        e_done, silu_step, hm_ready, hm_turned, hm_T_ready = (
            sem("e_done"), sem("silu_step"), sem("hm_ready"), sem("hm_turned"), sem("hm_T_ready"))
        y_ready, scattered, added = sem("y_ready"), sem("scattered"), sem("added")
        pick_step = sem("pick_step")
        dve_order, act_order, pool_order = sem("dve_order"), sem("act_order"), sem("pool_order")

        uses = [("ik", 0, "act")]
        uses += [("iq", k, "act") for k in range(4)]
        uses += [("dots", (0, jj, par), "act") for jj in range(2) for par in range(2)]
        uses += [("dots", (1, jj, par), "act") for jj in range(4) for par in range(2)]
        uses += [("ak", 0, "act")]
        uses += [("aq", k, "act") for k in range(4)]
        uses += [("rq", k, "act") for k in range(4)]
        units = [(th, pair) for th in range(TH) for pair in range(HEADS // 2)]
        attn = [[("s", u, "dve"), ("pt", u, "act"), ("o", u, "act")] for u in range(len(units))]
        uses += [attn[0][0], attn[1][0]]
        for u in range(len(units)):
            if u + 2 < len(units):
                uses.append(attn[u + 2][0])
            uses += attn[u][1:]
        uses += [("rk", k, "act") for k in range(4)]
        uses += [("rs", 0, "dve")]
        for hh in range(HEADS):
            if hh + 1 < HEADS:
                uses.append(("rs", hh + 1, "dve"))
            if hh % 2:
                uses.append(("ro", hh // 2, "act"))
        uses += [("rt", k, "act") for k in range(4)]
        number = {(kind, what): n for n, (kind, what, _) in enumerate(uses)}

        def freed(n):
            who = uses[n][2]
            return (act_freed if who == "act" else dve_freed), sum(1 for w in uses[:n + 1] if w[2] == who)

        def bank(kind, what):
            return ps[:, number[(kind, what)] % 8, :]

        def width(th):
            return (th + 1) * P

        block = ctx.enter_context(nc.Block())

        @block.sync
        def _(sp):
            sp.dma_start(xs[:, 0, :], x_v[0]).then_inc(x_in[0], 16)
            sp.dma_start(xs[:, 1, :], x_v[1]).then_inc(x_in[1], 16)

            def load(k, dst, src, wait):
                if wait is not None:
                    sp.wait_ge(ring_used, wait)
                sp.dma_start(dst, src).then_inc(landed[chunk_slot(k)], 16)

            def in_block(b, r, s, first):
                if not first:
                    b = sp.snap(b * NB)
                for q in range(BLOCK_CHUNKS):
                    k = BLOCK_CHUNKS * s + q
                    load(k, ring[:, chunk_slot(k), :].rearrange("p (c n) -> p c n", c=4),
                         w_in_v[:, 4 * q:4 * q + 4, bass.ds(b * NB if first else b, NB)],
                         None if first else r * RING + k - RING + 1)

            for s in range(3):
                in_block(s, 0, s, True)
            with sp.Fori(1, FULL // 3) as r:
                for s in range(3):
                    in_block(r * 3 + s, r, s, False)
            for s in range(FULL % 3):
                in_block(FULL - FULL % 3 + s, FULL // 3, s, False)
            load(TAIL_CHUNK, ring[:, chunk_slot(TAIL_CHUNK), 0:C * TAIL].rearrange("p (c n) -> p c n", c=C),
                 w_in_v[:, :, FULL * NB:IN_WIDTH], TAIL_CHUNK - RING + 1)
            for c in range(C):
                k = OUT_CHUNK + c
                load(k, ring[:, chunk_slot(k), :], w_out_v[c], k - RING + 1)

            def pair(it, number):
                for n in range(PAIR_CHUNKS):
                    k = MOE_CHUNK + n
                    if n < 16:
                        q, m = n // 4, n % 4
                        src = (w1_v if m < 2 else w3_v)[bass.ds(number * 2 + m % 2, 1), :, q * 2048:(q + 1) * 2048]
                    else:
                        q, m = (n - 16) // 2, n % 2
                        src = w2_v[bass.ds(number * 2 + m, 1), :, q * 2048:(q + 1) * 2048]
                    load(k, ring[:, chunk_slot(k), :], src.rearrange("o p n -> (o p) n"),
                         it * PAIR_CHUNKS + (k - RING + 1))

            with sp.Fori(0, PAIRS) as it:
                pair(it, it)
            sp.wait_ge(flag_ready, 1)
            over = sp.value_load(flag[0:1, 0:1], min_val=0, max_val=1)
            with sp.If(over > 0):
                with sp.Fori(1, PASSES) as pass_:
                    with sp.Fori(0, PAIRS) as number:
                        pair(pass_ * PAIRS + number, number)
                sp.wait_ge(added, 8 * (PASSES * PAIRS + 2))
            with sp.Else():
                sp.wait_ge(added, 8 * (PAIRS + 2))
            for th in range(TH):
                sp.dma_start(out_v[th], xs[:, th, :]).then_inc(stored, 16)
            sp.wait_ge(stored, 16 * TH)

        @block.gpsimd
        def _(pool):
            pool.dma_start(g_row, norm1_g.partition_broadcast(P).rearrange("p l n -> p (l n)")).then_inc(g1_in, 16)
            pool.dma_start(const[:, :], consts).then_inc(const_in, 16)
            pool.wait_ge(hT_full, 8)
            for dst, src in ((gain_q, q_norm_g), (gain_k, k_norm_g), (ln_w, idx_k_ln_w), (ln_b, idx_k_ln_b)):
                pool.dma_start(dst, src.partition_broadcast(P).rearrange("p l n -> p (l n)")).then_inc(gains_in, 16)
            n = 0
            pool.wait_ge(const_in, 16)
            pool.wait_ge(bank_free, 4 + 2 * 10)
            for th in range(TH):
                for part in (RQ, RK):
                    v = proj[:, th, part:part + 1024].rearrange("p (h a d) -> p h a d", h=HEADS, a=2)
                    cos = const[:, COS + th * 64:COS + th * 64 + 64].unsqueeze(1).broadcast_to([P, HEADS, 64])
                    sin = const[:, SIN + th * 64:SIN + th * 64 + 64].unsqueeze(1).broadcast_to([P, HEADS, 64])
                    t = [buf_a[:, i * 512:(i + 1) * 512].rearrange("p (h d) -> p h d", h=HEADS) for i in range(4)]
                    pool.tensor_tensor(t[0], v[:, :, 0, :], cos, ALU.mult)
                    pool.tensor_tensor(t[1], v[:, :, 1, :], sin, ALU.mult)
                    pool.tensor_tensor(t[2], v[:, :, 0, :], sin, ALU.mult)
                    pool.tensor_tensor(t[3], v[:, :, 1, :], cos, ALU.mult).then_inc(pool_order, 1)
                    n += 1
                    pool.wait_ge(pool_order, n)
                    pool.tensor_tensor(v[:, :, 0, :], t[0], t[1], ALU.subtract)
                    pool.tensor_tensor(v[:, :, 1, :], t[2], t[3], ALU.add).then_inc(rotated, 1)
                    pool.wait_ge(rotated, n)
            pool.wait_ge(prob_ready, len(units))
            pool.wait_ge(bank_full, number[("pt", len(units) - 1)] + 1)
            pool.dma_start(gain_r, ret_norm_g.partition_broadcast(P).rearrange("p l n -> p (l n)")).then_inc(ret_gain_in, 16)
            pool.wait_ge(ret_ready, 1)
            pool.wait_ge(bank_full, number[("ro", 3)] + 1)
            pool.dma_start(g2_row, norm2_g.partition_broadcast(P).rearrange("p l n -> p (l n)")).then_inc(g2_in, 16)
            pool.dma_start(stage_g, w_group.rearrange("l (p c) g -> (l p) c g", c=C)).then_inc(router_in, 16)
            for g in range(GROUPS):
                pool.dma_start(stage_r[:, g], w_router[0, g].rearrange("(p c) e -> p c e", c=C)).then_inc(router_in, 16)

        @block.scalar
        def _(act):
            order = [0]

            def norm_root(dst, src, n, wait):
                nc.scalar.activation(dst, src, ACT.Sqrt, bias=st[:, FLAG:FLAG + 1], scale=1.0 / n).then_inc(wait, 1)

            act.wait_ge(eps_set, 1)
            for th in range(TH):
                act.wait_ge(x_in[th], 16)
                nc.scalar.activation(h[:, th, :], xs[:, th, :], ACT.Square,
                                     accum_out=st[:, SSQ + th:SSQ + th + 1]).then_inc(ssq_done, 1)
                act.wait_ge(ssq_done, th + 1)
                norm_root(st[:, RSTD + th:RSTD + th + 1], st[:, SSQ + th:SSQ + th + 1], D, root_done)
            for k in range(0, 8, 2):
                act.wait_ge(hT_full, k + 1)
                nc.scalar.copy(hT[:, 2 * k:2 * k + 2, :].rearrange("p c t -> p (c t)"), ps[:, k, :]).then_inc(bank_free, 1)

            def out_of_bank(b_reg, s, n):
                for th in range(TH):
                    if th == 0:
                        act.wait_ge(block_done, b_reg + 1)
                    else:
                        act.wait_ge(ring_used, b_reg * BLOCK_CHUNKS + BLOCK_CHUNKS if n == NB else TAIL_CHUNK + 1)
                    nc.scalar.copy(proj[:, th, bass.ds(b_reg * NB, n)], ps[:, 2 * s + th, 0:n]).then_inc(bank_free, 1)

            with act.Fori(0, 2) as r:
                for s in range(3):
                    out_of_bank(r * 3 + s, s, NB)
            act.wait_ge(qk_ssq, 2)
            norm_root(st[:, QKR:QKR + 20], st[:, QKS:QKS + 20], HD, qk_root)
            act.wait_ge(qk_ssq, 3)
            norm_root(st[:, VAR:VAR + 2], st[:, MU + 2:MU + 4], ID, qk_root)
            with act.Fori(2, 4) as r:
                for s in range(3):
                    out_of_bank(r * 3 + s, s, NB)
            out_of_bank(12, 0, NB)
            out_of_bank(13, 1, TAIL)
            act.wait_ge(bank_free, 4 + 28)
            for th in range(TH):
                nc.scalar.activation(exp_g[:, th, :], proj[:, th, RG:RG + 1024], ACT.Exp, scale=-1.0).then_inc(silu_exp, 1)

            def take(kind, what, dst, extra=None, func=None):
                act.wait_ge(bank_full, number[(kind, what)] + 1)
                if extra is not None:
                    act.wait_ge(*extra)
                src = bank(kind, what)
                src = src[:, 0:dst.shape[-1]] if len(dst.shape) == 2 else src
                if func is None:
                    nc.scalar.copy(dst, src).then_inc(act_freed, 1)
                else:
                    nc.scalar.activation(dst, src, func).then_inc(act_freed, 1)

            def flat2(ap):
                return ap.rearrange("p c t -> p (c t)")

            act.wait_ge(rotated, 4)
            take("ik", 0, ikT)
            for k in range(4):
                take("iq", k, flat2(iqT[:, 2 * k:2 * k + 2, :]))
            n = 0
            for th, jn in ((0, 2), (1, 4)):
                for jj in range(jn):
                    for par in range(2):
                        take("dots", (th, jj, par), relu[:, n % 2, :], (relu_read, n - 1) if n >= 2 else None, ACT.Relu)
                        n += 1
            take("ak", 0, flat2(akT))
            act.wait_ge(silu_done, 1)
            for k in range(4):
                take("aq", k, flat2(aqT[:, 2 * k:2 * k + 2, :]))
            for k in range(4):
                take("rq", k, flat2(rqT[:, 2 * k:2 * k + 2, :]))

            def exps(u):
                th = units[u][0]
                act.wait_ge(scored, u + 1)
                for a in range(2):
                    last = nc.scalar.activation(prob[:, u % 2, a, 0:width(th)], prob[:, u % 2, a, 0:width(th)], ACT.Exp,
                                                bias=st[:, NEG + 2 * u + a:NEG + 2 * u + a + 1],
                                                accum_out=st[:, SUM + 2 * u + a:SUM + 2 * u + a + 1])
                last.then_inc(exp_done, 1)

            exps(0)
            for u, (th, pr) in enumerate(units):
                if u + 1 < len(units):
                    exps(u + 1)
                w = 4 * P if th else 2 * P
                take("pt", u, p_t[:, u % 2, 0:w])
                act.wait_ge(bank_full, number[("o", u)] + 1)
                nc.scalar.copy(mixedT(2 * pr, 2).rearrange("p (h t) -> p h t", h=2)[:, :, th * P:(th + 1) * P],
                               bank("o", u)[:, 0:2 * P].rearrange("p (h t) -> p h t", h=2)).then_inc(act_freed, 1)
            for k in range(4):
                take("rk", k, flat2(rkT[:, 2 * k:2 * k + 2, :]))

            for hh in range(HEADS):
                if hh >= 2:
                    act.wait_ge(inner_ready, hh - 1)
                nc.scalar.activation(decay[:, hh % 2, :], const[:, REL:REL + 256], ACT.Exp,
                                     scale=LOG_GAMMA[hh]).then_inc(decay_ready, 1)
                if hh % 2:
                    act.wait_ge(bank_full, number[("ro", hh // 2)] + 1)
                    k = RQ + (hh - 1) * HD
                    nc.scalar.copy(proj[:, :, k:k + 2 * HD].rearrange("p t (h d) -> p h t d", h=2),
                                   bank("ro", hh // 2).rearrange("p (h t d) -> p h t d", h=2, t=2)).then_inc(act_freed, 1)
            act.wait_ge(ret_ssq, 1)
            norm_root(st[:, RETR:RETR + 16], st[:, RETS:RETS + 16], HD, ret_root)
            for k in range(4):
                take("rt", k, mixedT(HEADS + 2 * k, 2))

            for th in range(TH):
                act.wait_ge(x2_done, 4 * th + 4)
                nc.scalar.activation(h[:, th, :], xs[:, th, :], ACT.Square,
                                     accum_out=st[:, SSQ + th:SSQ + th + 1]).then_inc(ssq_done, 1)
                act.wait_ge(ssq_done, TH + th + 1)
                norm_root(st[:, RSTD + th:RSTD + th + 1], st[:, SSQ + th:SSQ + th + 1], D, root_done)
            for k in range(0, 8, 2):
                act.wait_ge(hT_full, 8 + k + 1)
                nc.scalar.copy(hT[:, 2 * k:2 * k + 2, :].rearrange("p c t -> p (c t)"), ps[:, k, :]).then_inc(bank_free, 1)
            for th in range(TH):
                act.wait_ge(g_max, th + 1)
                nc.scalar.activation(g_exp[:, th, :], logit[:, th, 0:GROUPS], ACT.Exp, bias=small[:, th, 0:1],
                                     accum_out=small[:, th, 1:2]).then_inc(g_expd, 1)
            for th in range(TH):
                act.wait_ge(e_max, th + 1)
                nc.scalar.activation(small[:, th, 3:4], top8[:, th, 1, 1:2], ACT.Exp,
                                     bias=small[:, th, 2:3]).then_inc(e_expd, 1)

            def gathered(g):
                for j in range(4):
                    act.wait_ge(gather_done, g * 4 + (j + 1))
                    nc.scalar.copy(h_e[:, 4 * j:4 * j + 4, :].rearrange("p c s -> p (c s)"),
                                   ps[:, 2 + j % 2, :]).then_inc(h_e_ready, 1)

            act.wait_ge(mixed_done, 8)
            gathered(0)

            def pair(it):
                act.wait_ge(ring_used, it * PAIR_CHUNKS + (MOE_CHUNK + 16))
                nc.scalar.activation(e_sb, ps[:, 0, :], ACT.Exp, scale=-1.0).then_inc(e_done, 1)
                gathered(it + 1)
                act.wait_ge(hm_turned, it + 1)
                nc.scalar.copy(hm_T.rearrange("p j s -> p (j s)"), ps[:, 2, :]).then_inc(hm_T_ready, 1)
                act.wait_ge(gate_turned, it + 2)
                nc.scalar.copy(gate_T, ps[:, 3, 0:2 * P]).then_inc(gate_T_ready, 1)
                act.wait_ge(ring_used, it * PAIR_CHUNKS + (MOE_CHUNK + PAIR_CHUNKS))
                for n in range(4):
                    nc.scalar.copy(y_sb[:, n * NB:(n + 1) * NB], ps[:, 4 + n, :]).then_inc(y_ready, 1)

            with act.Fori(0, PAIRS) as it:
                pair(it)
            act.wait_ge(flag_ready, 1)
            over = act.value_load(flag[0:1, 0:1], min_val=0, max_val=1)
            with act.If(over > 0):
                with act.Fori(PAIRS, PASSES * PAIRS) as it:
                    pair(it)

        @block.vector
        def _(v):
            order = [0]

            def ordered(ins):
                order[0] += 1
                ins.then_inc(dve_order, 1)
                v.wait_ge(dve_order, order[0])

            V = nc.vector

            def normed(g, base):
                for th in range(TH):
                    v.wait_ge(root_done, base + th + 1)
                    ordered(V.reciprocal(st[:, RSTD + th:RSTD + th + 1], st[:, RSTD + th:RSTD + th + 1]))
                    V.scalar_tensor_tensor(h[:, th, :].rearrange("p (c q) -> p c q", c=C),
                                           xs[:, th, :].rearrange("p (q c) -> p c q", c=C),
                                           st[:, RSTD + th:RSTD + th + 1],
                                           g.rearrange("p (q c) -> p c q", c=C),
                                           ALU.mult, ALU.mult).then_inc(h_done, 1)

            V.memset(st[:, FLAG:FLAG + 1], EPS).then_inc(eps_set, 1)
            v.wait_ge(g1_in, 16)
            normed(g_row, 0)
            for k in range(1, 8, 2):
                v.wait_ge(hT_full, k + 1)
                V.tensor_copy(hT[:, 2 * k:2 * k + 2, :].rearrange("p c t -> p (c t)"), ps[:, k, :]).then_inc(hT_by_dve, 1)

            v.wait_ge(bank_free, 4 + 2 * 3)
            heads = HEADS + KV
            for th in range(TH):
                a = proj[:, th, AQ:AV]
                ordered(V.tensor_tensor(sq, a, a, ALU.mult))
                V.tensor_reduce(st[:, QKS + heads * th:QKS + heads * (th + 1)], sq.rearrange("p (h d) -> p h d", d=HD),
                                AX, ALU.add).then_inc(qk_ssq, 1)
                v.wait_ge(qk_ssq, th + 1)
            v.wait_ge(bank_free, 4 + 2 * 6)
            ik = proj[:, :, IK:IK + ID]
            ordered(V.tensor_reduce(st[:, MU:MU + 2], ik, AX, ALU.add))
            ordered(V.tensor_scalar(st[:, MU:MU + 2], st[:, MU:MU + 2], 1.0 / ID, None, ALU.mult))
            ordered(V.tensor_tensor(ik, ik, st[:, MU:MU + 2].unsqueeze(2).broadcast_to([P, TH, ID]), ALU.subtract))
            sq_i = sq[:, 0:TH * ID].rearrange("p (t d) -> p t d", t=TH)
            ordered(V.tensor_tensor(sq_i, ik, ik, ALU.mult))
            V.tensor_reduce(st[:, MU + 2:MU + 4], sq_i, AX, ALU.add).then_inc(qk_ssq, 1)
            iw = proj[:, :, IW:IW + IH]
            ordered(V.tensor_scalar(iw, iw, IH ** -0.5 * ID ** -0.5, None, ALU.mult))
            v.wait_ge(qk_root, 2)
            v.wait_ge(gains_in, 64)
            V.reciprocal(st[:, QKR:QKR + 20], st[:, QKR:QKR + 20])
            ordered(V.reciprocal(st[:, VAR:VAR + 2], st[:, VAR:VAR + 2]))
            for th in range(TH):
                a = proj[:, th, AQ:AV].rearrange("p (h d) -> p h d", d=HD)
                r = st[:, QKR + heads * th:QKR + heads * (th + 1)]
                ordered(V.tensor_tensor(a, a, r.unsqueeze(2).broadcast_to([P, heads, HD]), ALU.mult))
                V.tensor_tensor(a[:, 0:HEADS], a[:, 0:HEADS], gain_q.unsqueeze(1).broadcast_to([P, HEADS, HD]), ALU.mult)
                V.tensor_tensor(a[:, HEADS:heads], a[:, HEADS:heads], gain_k.unsqueeze(1).broadcast_to([P, KV, HD]),
                                ALU.mult).then_inc(qk_done, 1)
                ordered(V.scalar_tensor_tensor(ik[:, th], ik[:, th], st[:, VAR + th:VAR + th + 1], ln_w, ALU.mult, ALU.mult))
                V.tensor_tensor(ik_dup[:, th, 0:ID], ik[:, th], ln_b, ALU.add)
                V.tensor_tensor(ik_dup[:, th, ID:2 * ID], ik[:, th], ln_b, ALU.add).then_inc(index_ready, 1)
            v.wait_ge(silu_exp, 2)
            rg = proj[:, :, RG:RG + 1024]
            ordered(V.tensor_scalar(exp_g, exp_g, 1.0, None, ALU.add))
            ordered(V.reciprocal(exp_g, exp_g))
            V.tensor_tensor(rg, rg, exp_g, ALU.mult).then_inc(silu_done, 1)

            v.wait_ge(rotated, 4)
            ordered(V.memset(score, 0.0))
            n = 0
            for th, jn in ((0, 2), (1, 4)):
                w, per = width(th), NB // width(th)
                for jj in range(jn):
                    for par in range(2):
                        v.wait_ge(act_freed, freed(number[("dots", (th, jj, par))])[1])
                        for i in range(per):
                            head = 2 * (per * jj + i) + par
                            ins = V.scalar_tensor_tensor(score[:, th, 0:w], relu[:, n % 2, i * w:(i + 1) * w],
                                                         proj[:, th, IW + head:IW + head + 1], score[:, th, 0:w],
                                                         ALU.mult, ALU.add)
                            if i < per - 1:
                                ordered(ins)
                        ins.then_inc(relu_read, 1)
                        n += 1
                        v.wait_ge(relu_read, n)
            for th in range(TH):
                w = width(th)
                last = V.memset(score[0:CHUNK, th, w - CHUNK:w], HIDDEN)
            ordered(last)
            for _ in range(TOPK // 8):
                for th in range(TH):
                    w = width(th)
                    last = V.max(st[:, M8 + 8 * th:M8 + 8 * th + 8], score[:, th, 0:w])
                ordered(last)
                for th in range(TH):
                    w = width(th)
                    last = V.match_replace(score[:, th, 0:w], st[:, M8 + 8 * th:M8 + 8 * th + 8], score[:, th, 0:w], SENT)
                ordered(last)
            for th in range(TH):
                w = width(th)
                last = V.tensor_scalar(bias[:, th, 0:w], score[:, th, 0:w], SENT, OFF, ALU.is_gt, ALU.mult)
            ordered(last)

            def scores(u):
                th = units[u][0]
                w = width(th)
                v.wait_ge(bank_full, number[("s", u)] + 1)
                if u >= 2:
                    v.wait_ge(bank_full, number[("pt", u - 2)] + 1)
                s = bank("s", u).rearrange("p (h s) -> p h s", h=2)[:, :, 0:w]
                pr = prob[:, u % 2, :, 0:w]
                V.scalar_tensor_tensor(pr, s, HD ** -0.5, bias[:, th, 0:w].unsqueeze(1).broadcast_to([P, 2, w]),
                                       ALU.mult, ALU.add).then_inc(dve_freed, 1)
                v.wait_ge(dve_freed, freed(number[("s", u)])[1])
                m = st[:, NEG + 2 * u:NEG + 2 * u + 2]
                ordered(V.tensor_reduce(m, pr, AX, ALU.max))
                V.tensor_scalar(m, m, -1.0, None, ALU.mult).then_inc(scored, 1)

            def probs(u):
                th = units[u][0]
                w = width(th)
                v.wait_ge(exp_done, u + 1)
                r = st[:, RCP + 2 * u:RCP + 2 * u + 2]
                ordered(V.reciprocal(r, st[:, SUM + 2 * u:SUM + 2 * u + 2]))
                pr = prob[:, u % 2, :, 0:w]
                V.tensor_tensor(pr, pr, r.unsqueeze(2).broadcast_to([P, 2, w]), ALU.mult).then_inc(prob_ready, 1)

            scores(0)
            for u in range(len(units)):
                if u + 1 < len(units):
                    scores(u + 1)
                probs(u)

            for hh in range(HEADS):
                v.wait_ge(decay_ready, hh + 1)
                v.wait_ge(bank_full, number[("rs", hh)] + 1)
                if hh >= 2:
                    v.wait_ge(bank_full, number[("ro", hh // 2 - 1)] + 1)
                b = bank("rs", hh)
                V.scalar_tensor_tensor(inner[:, hh % 2, 0:256], b[:, 0:256], HD ** -0.5, decay[:, hh % 2, 0:256],
                                       ALU.mult, ALU.mult)
                ordered(V.scalar_tensor_tensor(inner[:, hh % 2, 256:384], b[:, 256:384], HD ** -0.5,
                                               decay[:, hh % 2, 0:128], ALU.mult, ALU.mult))
                v.sem_inc(dve_freed, 1)
                v.sem_inc(inner_ready, 1)
            v.wait_ge(act_freed, freed(number[("ro", 3)])[1])
            ret = proj[:, :, RQ:RQ + 1024]
            ordered(V.tensor_tensor(sq_r, ret, ret, ALU.mult))
            V.tensor_reduce(st[:, RETS:RETS + 16], sq_r.rearrange("p t (h d) -> p (t h) d", d=HD), AX,
                            ALU.add).then_inc(ret_ssq, 1)
            v.wait_ge(ret_gain_in, 16)
            ordered(V.tensor_tensor(rg, rg, gain_r.unsqueeze(1).broadcast_to([P, TH, 1024]), ALU.mult))
            v.wait_ge(ret_root, 1)
            ordered(V.reciprocal(st[:, RETR:RETR + 16], st[:, RETR:RETR + 16]))
            for th in range(TH):
                r4 = ret[:, th].rearrange("p (h d) -> p h d", d=HD)
                last = V.tensor_tensor(r4, r4, st[:, RETR + 8 * th:RETR + 8 * th + 8].unsqueeze(2).broadcast_to([P, HEADS, HD]),
                                       ALU.mult)
            ordered(last)
            V.tensor_tensor(ret, ret, rg, ALU.mult).then_inc(ret_ready, 1)
            v.wait_ge(router_in, 80)
            V.tensor_copy(gates_w[:, :, 0:GROUPS], stage_g)
            for g in range(GROUPS):
                last = V.tensor_copy(gates_w[:, :, GROUPS + g * 8:GROUPS + g * 8 + 8], stage_r[:, g])
            ordered(last)
            V.memset(g_pad[:], OFF)

            for i in range(8):
                th, n = i // 4, i % 4
                v.wait_ge(mixed_done, i + 1)
                xo = xs[:, th, n * NB:(n + 1) * NB]
                V.tensor_tensor(xo, xo, ps[:, i, :], ALU.add).then_inc(x2_done, 1)
            v.wait_ge(g2_in, 16)
            v.wait_ge(x2_done, 8)
            normed(g2_row, TH)
            for k in range(1, 8, 2):
                v.wait_ge(hT_full, 8 + k + 1)
                V.tensor_copy(hT[:, 2 * k:2 * k + 2, :].rearrange("p c t -> p (c t)"), ps[:, k, :]).then_inc(hT_by_dve, 1)

            v.wait_ge(logits_done, 1)
            ordered(V.tensor_copy(logit, ps[:, 0, 0:72].rearrange("p (t n) -> p t n", t=TH)))
            ordered(V.tensor_copy(g_pad[:, :, 0:GROUPS], logit[:, :, 0:GROUPS]))
            for th in range(TH):
                ordered(V.max(top8[:, th, 0, :], g_pad[:, th, :]))
                V.tensor_scalar(small[:, th, 0:1], top8[:, th, 0, 0:1], -1.0, None, ALU.mult).then_inc(g_max, 1)
                ordered(V.max_index(idx8[:, th, 0, :], top8[:, th, 0, :], g_pad[:, th, :]))
            ordered(V.tensor_copy(idxf[:, :, 0, :], idx8[:, :, 0, :]))
            for th in range(TH):
                ordered(V.tensor_scalar(oh[:, th, 0, :], iota[:, 0:8], idxf[:, th, 0, 0:1], None, ALU.is_equal))
            for th in range(TH):
                last = V.tensor_tensor(pick[:, th], logit[:, th, GROUPS:36].rearrange("p (g n) -> p g n", g=GROUPS),
                                       oh[:, th, 0, 0:GROUPS].unsqueeze(2).broadcast_to([P, GROUPS, 8]), ALU.mult)
            ordered(last)
            for th in range(TH):
                last = V.tensor_reduce(e_sel[:, th], pick[:, th].rearrange("p g n -> p n g"), AX, ALU.add)
            ordered(last)
            for th in range(TH):
                ordered(V.max(top8[:, th, 1, :], e_sel[:, th]))
                V.tensor_scalar(small[:, th, 2:3], top8[:, th, 1, 0:1], -1.0, None, ALU.mult).then_inc(e_max, 1)
                ordered(V.max_index(idx8[:, th, 1, :], top8[:, th, 1, :], e_sel[:, th]))
            ordered(V.tensor_copy(idxf[:, :, 1, :], idx8[:, :, 1, :]))
            for th in range(TH):
                for a in range(2):
                    last = V.tensor_scalar(oh[:, th, 1 + a, :], iota[:, 0:8], idxf[:, th, 1, a:a + 1], None, ALU.is_equal)
            ordered(last)
            V.tensor_tensor(cs[:, :, 1, :], oh[:, :, 1, :], oh[:, :, 2, :], ALU.add)
            v.wait_ge(g_expd, 2)
            v.wait_ge(e_expd, 2)
            ordered(V.tensor_scalar(small[:, :, 4:5], small[:, :, 3:4], 1.0, None, ALU.add))
            ordered(V.tensor_tensor(small[:, :, 4:5], small[:, :, 4:5], small[:, :, 1:2], ALU.mult))
            ordered(V.reciprocal(small[:, :, 5:6], small[:, :, 4:5]))
            ordered(V.tensor_tensor(small[:, :, 6:7], small[:, :, 5:6], small[:, :, 3:4], ALU.mult))
            for th in range(TH):
                ordered(V.tensor_scalar(cs[:, th, 0, :], oh[:, th, 1, :], small[:, th, 5:6], None, ALU.mult))
                ordered(V.scalar_tensor_tensor(cs[:, th, 0, :], oh[:, th, 2, :], small[:, th, 6:7], cs[:, th, 0, :],
                                               ALU.mult, ALU.add))
                for dst, a in ((comb, 0), (sel, 1)):
                    last = V.tensor_tensor(dst[:, th].rearrange("p (g n) -> p g n", g=GROUPS),
                                           oh[:, th, 0, 0:GROUPS].unsqueeze(2).broadcast_to([P, GROUPS, 8]),
                                           cs[:, th, a, :].unsqueeze(1).broadcast_to([P, GROUPS, 8]), ALU.mult)
            last.then_inc(sel_ready, 1)
            v.wait_ge(sel_ready, 1)
            v.wait_ge(ranks_done, 1)
            ordered(V.tensor_scalar(posm, ps[:, 1, 0:64].rearrange("p (t e) -> p t e", t=TH), 1.0, None, ALU.add))
            ordered(V.tensor_tensor(posm, posm, sel, ALU.mult))
            ordered(V.tensor_scalar(posm, posm, -1.0, None, ALU.add))
            ordered(V.tensor_reduce(small[:, 0, 7:8], ps[:, 1, 64:96], AX, ALU.max))
            V.tensor_scalar(flag[:, :], small[:, 0, 7:8], float(SLOTS), None, ALU.is_gt).then_inc(flag_ready, 1)
            V.memset(y_sb, 0.0).then_inc(y_ready, 4)
            V.memset(gate_T, 0.0).then_inc(gate_T_ready, 1)
            v.sem_inc(added, 8)
            v.sem_inc(gate_turned, 1)

            def slots(src, g):
                pass_, pr = (g >> 4) & (PASSES - 1), g & (PAIRS - 1)
                it = iota[:, bass.ds(pass_ * SLOTS, SLOTS)].unsqueeze(1).unsqueeze(1).broadcast_to([P, TH, 2, SLOTS])
                col = src[:, :, bass.ds(pr * 2, 2)].unsqueeze(3).broadcast_to([P, TH, 2, SLOTS])
                return it, col

            def pick_tokens(g):
                it, col = slots(posm, g)
                V.tensor_tensor(pick_p, col, it, ALU.is_equal).then_inc(pick_ready, 1)

            pick_tokens(0 * SLOTS)

            def pair(it):
                v.wait_ge(gate_turned, it + 1)
                i, col = slots(posm, it)
                V.tensor_tensor(gate_p, col, i, ALU.is_equal).then_inc(pick_step, 1)
                v.wait_ge(pick_step, it + 1)
                V.tensor_tensor(gate_p, gate_p, slots(comb, it)[1], ALU.mult).then_inc(gate_ready, 1)
                v.wait_ge(gather_done, it * 4 + 4)
                pick_tokens(it + 1)
                v.wait_ge(e_done, it + 1)
                V.tensor_scalar(e_sb, e_sb, 1.0, None, ALU.add).then_inc(silu_step, 1)
                v.wait_ge(silu_step, it * 3 + 1)
                V.reciprocal(e_sb, e_sb).then_inc(silu_step, 1)
                v.wait_ge(silu_step, it * 3 + 2)
                V.tensor_tensor(e_sb, e_sb, ps[:, 0, :], ALU.mult).then_inc(silu_step, 1)
                v.wait_ge(silu_step, it * 3 + 3)
                V.tensor_tensor(hm.rearrange("p (j q) -> p j q", j=J), e_sb.rearrange("p (q j) -> p j q", j=J),
                                ps[:, 1, :].rearrange("p (q j) -> p j q", j=J), ALU.mult).then_inc(hm_ready, 1)
                add_scattered(it)

            def add_scattered(it):
                for s in range(8):
                    v.wait_ge(scattered, it * 8 + (s + 1))
                    th, n = s // 4, s % 4
                    xo = xs[:, th, n * NB:(n + 1) * NB]
                    V.tensor_tensor(xo, xo, ps[:, 3 - s % 2, :], ALU.add).then_inc(added, 1)

            with v.Fori(0, PAIRS) as it:
                pair(it)
            v.wait_ge(flag_ready, 1)
            over = v.value_load(flag[0:1, 0:1], min_val=0, max_val=1)
            with v.If(over > 0):
                with v.Fori(PAIRS, PASSES * PAIRS) as it:
                    pair(it)
                add_scattered(PASSES * PAIRS)
            with v.Else():
                add_scattered(PAIRS)

        @block.tensor
        def _(pe):
            mm = nc.tensor.matmul

            def turn_h(base, ready):
                for k in range(8):
                    for cc in range(2):
                        for th in range(TH):
                            if k == 0 and cc == 0:
                                pe.wait_ge(h_done, ready + th + 1)
                            c = 2 * k + cc
                            last = nc.tensor.transpose(ps[:, k, (2 * cc + th) * P:(2 * cc + th + 1) * P],
                                                       h[:, th, c * P:(c + 1) * P], ident)
                    last.then_inc(hT_full, 1)
                pe.wait_ge(bank_free, base)
                pe.wait_ge(hT_by_dve, base - 28 if base > 28 else 4)

            pe.wait_ge(const_in, 16)
            turn_h(4, 0)

            def in_block(b, r, s, first, n=NB, chunks=BLOCK_CHUNKS):
                for th in range(TH):
                    if not first:
                        pe.wait_ge(bank_free, 2 * b + th - 1)
                    for c in range(C):
                        k = BLOCK_CHUNKS * s + c // 4 if chunks > 1 else BLOCK_CHUNKS * s
                        if th == 0 and c % 4 == 0 and (chunks > 1 or c == 0):
                            pe.wait_ge(landed[chunk_slot(k)], 16 * (r + 1))
                        per = C // chunks
                        last = mm(ps[:, 2 * s + th, 0:n], hT[:, c, th * P:(th + 1) * P],
                                  ring[:, chunk_slot(k), (c % per) * n:(c % per) * n + n],
                                  start=(c == 0), stop=(c == C - 1))
                        if th == TH - 1 and c % per == per - 1:
                            last.then_inc(ring_used, 1)
                    if th == 0:
                        last.then_inc(block_done, 1)

            for s in range(3):
                in_block(s, 0, s, True)
            with pe.Fori(1, FULL // 3) as r:
                for s in range(3):
                    in_block(r * 3 + s, r, s, False)
            in_block(12, 4, 0, False)
            in_block(13, 4, 1, False, TAIL, 1)

            def fill(kind, what):
                n = number[(kind, what)]
                if n >= 8:
                    pe.wait_ge(*freed(n - 8))
                elif n == 0:
                    pe.wait_ge(bank_free, 4 + 28)
                return ps[:, n % 8, :]

            def turn(kind, what, pieces):
                b = fill(kind, what)
                for i, piece in enumerate(pieces):
                    last = nc.tensor.transpose(b[:, i * P:(i + 1) * P], piece, ident)
                last.then_inc(bank_full, 1)

            def head_pair(part, k):
                return [proj[:, th, part + hh * HD:part + (hh + 1) * HD] for hh in (2 * k, 2 * k + 1) for th in range(TH)]

            pe.wait_ge(index_ready, 2)
            turn("ik", 0, [ik_dup[:, th, :] for th in range(TH)])
            for k in range(4):
                turn("iq", k, head_pair(IQ, k))
            pe.wait_ge(act_freed, 5)
            for th, jn in ((0, 2), (1, 4)):
                w = width(th)
                per = NB // w
                for jj in range(jn):
                    banks = [fill("dots", (th, jj, par)) for par in range(2)]
                    for i in range(per):
                        for par in range(2):
                            rows = slice(ID * par, ID * par + ID)
                            last = mm(banks[par][:, i * w:(i + 1) * w], iqT[rows, per * jj + i, th * P:(th + 1) * P],
                                      ikT[rows, 0:w], start=True, stop=True)
                    last.then_inc(bank_full, 2)
            pe.wait_ge(qk_done, 2)
            turn("ak", 0, head_pair(AK, 0))
            for k in range(4):
                turn("aq", k, head_pair(AQ, k))
            pe.wait_ge(rotated, 4)
            for k in range(4):
                turn("rq", k, head_pair(RQ, k))

            def scores(u):
                th, pr = units[u]
                b = fill("s", u)
                for a in range(2):
                    last = mm(b[:, a * 256:a * 256 + width(th)], aqT[:, 2 * pr + a, th * P:(th + 1) * P],
                              akT[:, pr // 2, 0:width(th)], start=True, stop=True)
                last.then_inc(bank_full, 1)

            pe.wait_ge(act_freed, freed(number[("aq", 3)])[1])
            scores(0)
            scores(1)
            for u, (th, pr) in enumerate(units):
                if u + 2 < len(units):
                    scores(u + 2)
                b = fill("pt", u)
                pe.wait_ge(prob_ready, u + 1)
                for a in range(2):
                    for sh in range(th + 1):
                        i = a * (th + 1) + sh
                        last = nc.tensor.transpose(b[:, i * P:(i + 1) * P], prob[:, u % 2, a, sh * P:(sh + 1) * P], ident)
                last.then_inc(bank_full, 1)
                b = fill("o", u)
                pe.wait_ge(*freed(number[("pt", u)]))
                for a in range(2):
                    for sh in range(th + 1):
                        i = a * (th + 1) + sh
                        last = mm(b[:, a * P:(a + 1) * P], proj[:, sh, AV + (pr // 2) * HD:AV + (pr // 2 + 1) * HD],
                                  p_t[:, u % 2, i * P:(i + 1) * P], start=(sh == 0), stop=(sh == th))
                last.then_inc(bank_full, 1)
            for k in range(4):
                turn("rk", k, head_pair(RK, k))
            pe.wait_ge(*freed(number[("rk", 3)]))

            def ret_scores(hh):
                b = fill("rs", hh)
                mm(b[:, 0:256], rkT[:, hh, 0:P], rqT[:, hh, :], start=True, stop=True)
                mm(b[:, 256:384], rkT[:, hh, P:2 * P], rqT[:, hh, P:2 * P], start=True, stop=True).then_inc(bank_full, 1)

            ret_scores(0)
            for hh in range(HEADS):
                if hh + 1 < HEADS:
                    ret_scores(hh + 1)
                if hh % 2:
                    b = fill("ro", hh // 2)
                    pe.wait_ge(inner_ready, hh + 1)
                    for a in range(2):
                        s = inner[:, a, :]
                        rv = [proj[:, th, RV + (hh - 1 + a) * HD:RV + (hh + a) * HD] for th in range(TH)]
                        mm(b[:, a * 256:a * 256 + P], s[:, 0:P], rv[0], start=True, stop=True)
                        mm(b[:, a * 256 + P:a * 256 + 2 * P], s[:, P:2 * P], rv[0], start=True, stop=False)
                        last = mm(b[:, a * 256 + P:a * 256 + 2 * P], s[:, 2 * P:3 * P], rv[1], start=False, stop=True)
                    last.then_inc(bank_full, 1)
            pe.wait_ge(ret_ready, 1)
            for k in range(4):
                turn("rt", k, head_pair(RQ, k))

            for n in range(len(uses) - 8, len(uses)):
                pe.wait_ge(*freed(n))
            for c in range(C):
                k = OUT_CHUNK + c
                pe.wait_ge(landed[chunk_slot(k)], chunk_landed(k))
                for i in range(8):
                    th, n = i // 4, i % 4
                    last = mm(ps[:, i, :], mixedT(c)[:, th * P:(th + 1) * P],
                              ring[:, chunk_slot(k), n * NB:(n + 1) * NB], start=(c == 0), stop=(c == C - 1))
                    if c == C - 1:
                        last.then_inc(mixed_done, 1)
                if c < C - 1:
                    last.then_inc(ring_used, 1)
            pe.wait_ge(mixed_done, 8)
            pe.sem_inc(ring_used, 1)

            pe.wait_ge(x2_done, 8)
            turn_h(4 + 28 + 4, 2)
            for th in range(TH):
                for c in range(C):
                    last = mm(ps[:, 0, th * 36:th * 36 + 36], hT[:, c, th * P:(th + 1) * P], gates_w[:, c, :],
                              start=(c == 0), stop=(c == C - 1))
            last.then_inc(logits_done, 1)
            pe.wait_ge(sel_ready, 1)
            mm(ps[:, 1, 0:32], before, sel[:, 0, :], start=True, stop=True)
            mm(ps[:, 1, 32:64], ones, sel[:, 0, :], start=True, stop=False)
            mm(ps[:, 1, 32:64], before, sel[:, 1, :], start=False, stop=True)
            mm(ps[:, 1, 64:96], ones, sel[:, 0, :], start=True, stop=False)
            mm(ps[:, 1, 64:96], ones, sel[:, 1, :], start=False, stop=True).then_inc(ranks_done, 1)

            def gather(g, waits):
                pe.wait_ge(pick_ready, g + 1)
                for j in range(4):
                    waits(j)
                    for c in range(4 * j, 4 * j + 4):
                        for th in range(TH):
                            last = mm(ps[:, 2 + j % 2, (c % 4) * P:(c % 4 + 1) * P], h[:, th, c * P:(c + 1) * P],
                                      pick_p[:, th].rearrange("p e s -> p (e s)"), start=(th == 0), stop=(th == TH - 1))
                    last.then_inc(gather_done, 1)

            def wait_copied(base):
                def waits(j):
                    if j >= 2:
                        pe.wait_ge(h_e_ready, base + (j - 1))
                return waits

            gather(0, wait_copied(0))

            def scatter(it):
                pe.wait_ge(y_ready, it * 4 + 4)
                pe.wait_ge(gate_T_ready, it + 1)
                for s in range(8):
                    if s == 1:
                        pe.wait_ge(hm_T_ready, it + 1)
                    if s >= 2:
                        pe.wait_ge(added, it * 8 + (8 + s - 1))
                    th, n = s // 4, s % 4
                    mm(ps[:, 3 - s % 2, :], gate_T[:, th * P:(th + 1) * P], y_sb[:, n * NB:(n + 1) * NB],
                       start=True, stop=True).then_inc(scattered, 1)

            def landed_now(it, n):
                k = MOE_CHUNK + n
                pe.wait_ge(landed[chunk_slot(k)], it * (16 * PAIR_CHUNKS // RING) + chunk_landed(k))
                return ring[:, chunk_slot(k), :]

            def pair(it):
                pe.wait_ge(h_e_ready, it * 4 + 4)
                for q in range(4):
                    w = [landed_now(it, 4 * q + m) for m in range(4)]
                    for cc in range(4):
                        c = 4 * q + cc
                        for m in range(4):
                            half = slice(SLOTS * (m % 2), SLOTS * (m % 2 + 1))
                            last = mm(ps[half, m // 2, :], h_e[:, c, half], w[m][:, cc * NB:(cc + 1) * NB],
                                      start=(c == 0), stop=(c == C - 1))
                    last.then_inc(ring_used, 4)

                def waits(j):
                    if j == 0:
                        pe.wait_ge(added, it * 8 + 8)
                    elif j == 1:
                        pe.wait_ge(gate_T_ready, it + 1)
                    else:
                        pe.wait_ge(h_e_ready, it * 4 + (4 + j - 1))
                gather(it + 1, waits)
                pe.wait_ge(hm_ready, it + 1)
                pe.wait_ge(h_e_ready, it * 4 + 7)
                for j in range(J):
                    last = nc.tensor.transpose(ps[:, 2, j * P:(j + 1) * P], hm[:, j * P:(j + 1) * P], ident)
                last.then_inc(hm_turned, 1)
                pe.wait_ge(h_e_ready, it * 4 + 8)
                scatter(it)
                pe.wait_ge(gate_ready, it + 1)
                pe.wait_ge(added, it * 8 + 15)
                for th in range(TH):
                    last = nc.tensor.transpose(ps[:, 3, th * P:(th + 1) * P],
                                               gate_p[:, th].rearrange("p e s -> p (e s)"), ident)
                last.then_inc(gate_turned, 1)
                for j in range(J):
                    w = [landed_now(it, 16 + 2 * j + m) for m in range(2)]
                    for n in range(4):
                        for m in range(2):
                            half = slice(SLOTS * m, SLOTS * (m + 1))
                            last = mm(ps[half, 4 + n, :], hm_T[:, j, half], w[m][:, n * NB:(n + 1) * NB],
                                      start=(j == 0), stop=(j == J - 1))
                    last.then_inc(ring_used, 2)

            with pe.Fori(0, PAIRS) as it:
                pair(it)

            def last_scatter(it):
                pe.wait_ge(y_ready, it * 4 + 4)
                pe.wait_ge(gate_T_ready, it + 1)
                pe.wait_ge(added, it * 8 + 8)
                for s in range(8):
                    if s >= 2:
                        pe.wait_ge(added, it * 8 + (8 + s - 1))
                    th, n = s // 4, s % 4
                    mm(ps[:, 3 - s % 2, :], gate_T[:, th * P:(th + 1) * P], y_sb[:, n * NB:(n + 1) * NB],
                       start=True, stop=True).then_inc(scattered, 1)

            pe.wait_ge(flag_ready, 1)
            over = pe.value_load(flag[0:1, 0:1], min_val=0, max_val=1)
            with pe.If(over > 0):
                with pe.Fori(PAIRS, PASSES * PAIRS) as it:
                    pair(it)
                last_scatter(PASSES * PAIRS)
            with pe.Else():
                last_scatter(PAIRS)


def constants():
    t = np.zeros((P, CONSTS), np.float32)
    p = np.arange(P)
    t[:, IDENT:IDENT + P] = np.eye(P)
    t[:, BEFORE:BEFORE + P] = p[:, None] < p[None, :]
    t[:, ONES:ONES + P] = 1.0
    inv = np.float32(1.0) / (np.float32(10000.0) ** np.linspace(0.0, 1.0, HD // 2, dtype=np.float32))
    ang = (np.arange(SEQ, dtype=np.float32)[:, None] * inv[None, :]).astype(np.float32)
    for th in range(TH):
        a = ang[th * P:(th + 1) * P]
        t[:, COS + th * 64:COS + th * 64 + 64] = np.cos(a)
        t[:, SIN + th * 64:SIN + th * 64 + 64] = np.sin(a)
    rel = np.arange(256)[None, :] - p[:, None]
    t[:, REL:REL + 256] = np.where(rel >= 0, rel, 1e9)
    t[:, IOTA:IOTA + SEQ] = np.arange(SEQ)
    return t


NAMES = ["x", "norm1_g", "w_in", "q_norm_g", "k_norm_g", "idx_k_ln_w", "idx_k_ln_b", "ret_norm_g", "w_out",
         "norm2_g", "w_group", "w_router", "w1", "w3", "w2"]


def kernel(**inputs):
    import concourse.bacc as bacc
    from concourse.bass_utils import run_bass_kernel_spmd

    nc = bacc.Bacc("TRN2", target_bir_lowering=False, num_devices=1)
    arrays = {f"{name}_dram": np.ascontiguousarray(inputs[name]) for name in NAMES}
    arrays["consts_dram"] = constants()
    args = [nc.dram_tensor(name, a.shape, F32, kind="ExternalInput").ap() for name, a in arrays.items()]
    out = nc.dram_tensor("out_dram", [1, SEQ, D], F32, kind="ExternalOutput").ap()
    build(nc, *args, out)
    r = run_bass_kernel_spmd(nc, [arrays], core_ids=[0])
    return r.results[0]["out_dram"]
```

```python
import math
from contextlib import ExitStack

import numpy as np

import concourse.bass as bass
from concourse import mybir

F32 = mybir.dt.float32
F32R = mybir.dt.float32r
I32 = mybir.dt.int32
U32 = mybir.dt.uint32
ALU = mybir.AluOpType
ACT = mybir.ActivationFunctionType
AX = mybir.AxisListType.X

P = 128
SEQ, D = 256, 2048
TH = SEQ // P
C = D // P
CHUNK = 64
HEADS, HD, KV = 8, 128, 2
IH, ID = 16, 64
TOPK = min(256, SEQ // 4)
GROUPS, PER_GROUP = 4, 8
EXPERTS, FF = 32, 512
J = FF // P
EPS = 1e-6
IN_WIDTH = 1024 + 256 + 256 + 1024 + 64 + 16 + 4 * 1024
AQ, AK, AV, IQ, IK, IW, RQ, RK, RV, RG = 0, 1024, 1280, 1536, 2560, 2624, 2640, 3664, 4688, 5712
NB = 512
BLOCKS = 14
BW = 2 * -(-IN_WIDTH // (2 * BLOCKS))
SLOTS = 64
PAIRS = EXPERTS // 2
PASSES = SEQ // SLOTS
SENT, HIDDEN, OFF = -3.0e38, -1.0e38, -1.0e30

ORDER = [3, 4, 5, 0, 1, 2] + list(range(6, BLOCKS))
BLOCK_UNITS = 8
UNITS = BLOCK_UNITS * BLOCKS
RAW = 4
SPLIT = 4

RING = 12
OUT_CHUNK = 0
MOE_CHUNK = C
PAIR_CHUNKS = 24

IDENT, BEFORE, ONES, COS, SIN, REL, IOTA = 0, 128, 256, 384, 512, 640, 896
CONSTS = IOTA + SEQ
SSQ, RSTD, QKS, QKR, MU, VAR, M8, NEG, SUM, RCP, RETS, RETR, EPS_AT, SSQ2, RSTD2 = (
    0, 2, 4, 24, 44, 48, 52, 68, 84, 100, 116, 132, 148, 150, 154)
LOG_GAMMA = [math.log1p(-2.0 ** (-5 - h)) for h in range(HEADS)]


def chunk_slot(k):
    return (k + 8) % RING


def chunk_landed(k):
    return 16 * (k // RING + 1)


def build(nc, x, norm1_g, w_in, q_norm_g, k_norm_g, idx_k_ln_w, idx_k_ln_b, ret_norm_g, w_out,
          norm2_g, w_group, w_router, w1, w3, w2, consts, out):
    ctx = ExitStack()
    with ctx:
        def sb(name, shape, dt=F32):
            return ctx.enter_context(nc.sbuf_tensor(name, shape, dt))

        def sem(name):
            return ctx.enter_context(nc.semaphore(name))

        base = (nc.sbuf_base + 31) // 32 * 32
        ring = sb("ring", [P, RING, 2048])
        zT_hi, zT_lo, w_hi, w_lo = (
            nc.alloc_sbuf_tensor_at(name, [P, 4096], F32R, offset=base + i * 4 * 4096)
            for i, name in enumerate(("zT_hi", "zT_lo", "w_hi", "w_lo")))
        xs = sb("xs", [P, TH, D])
        flat = sb("flat", [P, TH * IN_WIDTH])
        buf_a = sb("buf_a", [P, 4096])
        buf_b = sb("buf_b", [P, 4096])
        const = sb("const", [P, CONSTS])
        st = sb("st", [P, 160])
        flag = sb("flag", [P, 1], I32)
        idx8 = sb("idx8", [P, TH, 2, 8], U32)
        p_t = sb("p_t", [P, 2, 512])
        ps = ctx.enter_context(nc.psum_tensor("ps", [P, 8, 512], F32))

        proj = flat[:, :].rearrange("p (t n) -> p t n", t=TH)
        ident = const[:, IDENT:IDENT + P]
        before = const[:, BEFORE:BEFORE + P]
        ones = const[:, ONES:ONES + P]
        iota = const[:, IOTA:IOTA + SEQ]

        z = buf_a[:, :].rearrange("p (t n) -> p t n", t=TH)
        zT = buf_b[:, :].rearrange("p (c t) -> p c t", c=C)
        g_row = flat[:, 0:D]
        g2_row = flat[:, RV:RV + D]
        rot = buf_a[:, 0:2048].rearrange("p (a h d) -> p a h d", a=4, h=HEADS)
        sq = buf_a[:, 0:2 * 1280].rearrange("p (t n) -> p t n", t=TH)
        gain_q = buf_a[:, 3328:3456]
        gain_k = buf_a[:, 3456:3584]
        ln_w = buf_a[:, 3584:3648]
        ln_b = buf_a[:, 3648:3712]
        ik_dup = buf_a[:, 3712:3968].rearrange("p (t n) -> p t n", t=TH)
        prob = buf_a[:, 2048:4096].rearrange("p (b h s) -> p b h s", b=4, h=2)
        inner = buf_a[:, 0:3072].rearrange("p (b n) -> p b n", b=HEADS)
        decay = buf_a[:, 3072:4096].rearrange("p (b n) -> p b n", b=4)
        relu = buf_b[:, 0:2048].rearrange("p (b n) -> p b n", b=4)
        aqT = buf_b[:, 0:2048].rearrange("p (h t) -> p h t", h=HEADS)
        iqT = buf_b[:, 2048:4096].rearrange("p (h t) -> p h t", h=IH // 2)
        rkT, rqT = aqT, iqT
        sq_r = buf_b[:, 0:2048].rearrange("p (t n) -> p t n", t=TH)
        akT = flat[:, IQ:IQ + 512].rearrange("p (h t) -> p h t", h=KV)
        bias = flat[:, IQ + 512:IQ + 1024].rearrange("p (t s) -> p t s", t=TH)
        exp_g = proj[:, :, IQ:IQ + 1024]
        ikT = p_t[:, 0, 0:256]
        score = p_t[:, 1, :].rearrange("p (t s) -> p t s", t=TH)
        gain_r = p_t[:, :, :].rearrange("p b n -> p (b n)")

        def mixedT(c, n=1):
            base = (IN_WIDTH if c % 8 >= 4 else 0) + (IQ if c >= HEADS else 0) + (c % 4) * SEQ
            return flat[:, base:base + n * SEQ]

        rb = IN_WIDTH + RV
        gates_w = flat[:, rb:rb + C * 36].rearrange("p (c n) -> p c n", c=C)
        stage_g = flat[:, rb + 576:rb + 640].rearrange("p (c n) -> p c n", c=C)
        stage_r = flat[:, rb + 640:rb + 1152].rearrange("p (g c n) -> p g c n", g=GROUPS, c=C)
        logit = flat[:, rb + 1152:rb + 1224].rearrange("p (t n) -> p t n", t=TH)
        g_pad = flat[:, rb + 1224:rb + 1240].rearrange("p (t n) -> p t n", t=TH)
        g_exp = flat[:, rb + 1240:rb + 1248].rearrange("p (t n) -> p t n", t=TH)
        pick = flat[:, rb + 1248:rb + 1312].rearrange("p (t g n) -> p t g n", t=TH, g=GROUPS)
        e_sel = flat[:, rb + 1312:rb + 1328].rearrange("p (t n) -> p t n", t=TH)
        top8 = flat[:, rb + 1328:rb + 1360].rearrange("p (t a n) -> p t a n", t=TH, a=2)
        idxf = flat[:, rb + 1360:rb + 1392].rearrange("p (t a n) -> p t a n", t=TH, a=2)
        oh = flat[:, rb + 1392:rb + 1440].rearrange("p (t a n) -> p t a n", t=TH, a=3)
        cs = flat[:, rb + 1440:rb + 1472].rearrange("p (t a n) -> p t a n", t=TH, a=2)
        small = flat[:, rb + 1472:rb + 1488].rearrange("p (t n) -> p t n", t=TH)
        comb = flat[:, rb + 1488:rb + 1552].rearrange("p (t e) -> p t e", t=TH)
        sel = flat[:, rb + 1552:rb + 1616].rearrange("p (t e) -> p t e", t=TH)
        posm = flat[:, rb + 1616:rb + 1680].rearrange("p (t e) -> p t e", t=TH)

        h_e = flat[:, 0:2048].rearrange("p (c s) -> p c s", c=C)
        y_sb = flat[:, 2048:4096]
        pick_p = flat[:, 6800:7056].rearrange("p (t e s) -> p t e s", t=TH, e=2)
        gate_p = flat[:, 7056:7312].rearrange("p (t e s) -> p t e s", t=TH, e=2)
        gate_T = flat[:, 7312:7568]
        e_sb = flat[:, 7568:8080]
        hm = flat[:, 8080:8592]
        hm_T = flat[:, 8592:9104].rearrange("p (j s) -> p j s", j=J)

        x_v = x.rearrange("b (t p) d -> (b t) p d", p=P)
        out_v = out.rearrange("b (t p) d -> (b t) p d", p=P)
        w_in_v = w_in.rearrange("l (p c) n -> (l p) c n", c=C)
        w_out_v = w_out.rearrange("l (c p) n -> p (l c) n", p=P)
        w1_v = w1.rearrange("l e (p c) f -> (l e) p (c f)", c=C)
        w3_v = w3.rearrange("l e (p c) f -> (l e) p (c f)", c=C)
        w2_v = w2.rearrange("l e (p j) n -> (l e) p (j n)", j=J)

        landed = [sem(f"landed{i}") for i in range(RING)]
        x_in = [sem("x_in0"), sem("x_in1")]
        const_in, g1_in, gains_in = sem("const_in"), sem("g1_in"), sem("gains_in")
        ret_gain_in, g2_in, router_in = sem("ret_gain_in"), sem("g2_in"), sem("router_in")
        stored = sem("stored")
        ring_used = sem("ring_used")
        raw_landed = [sem(f"raw_landed{i}") for i in range(RAW)]
        hi_done, lo_done = sem("hi_done"), sem("lo_done")
        unit_used = sem("unit_used")
        z_done, z_turned = sem("z_done"), sem("z_turned")
        zT_hi_done, zT_lo_done = sem("zT_hi_done"), sem("zT_lo_done")
        zT_by_act, zT_by_dve = sem("zT_by_act"), sem("zT_by_dve")
        ssq_done, root_done, rstd_ready = sem("ssq_done"), sem("root_done"), sem("rstd_ready")
        evacuated = sem("evacuated")
        qk_ssq, qk_root, qk_done = sem("qk_ssq"), sem("qk_root"), sem("qk_done")
        qk_squared, qk_scaled = sem("qk_squared"), sem("qk_scaled")
        ik_var, ik_root = sem("ik_var"), sem("ik_root")
        eps_set = sem("eps_set")
        index_ready, rotated, silu_exp, silu_done = sem("index_ready"), sem("rotated"), sem("silu_exp"), sem("silu_done")
        bank_full, act_freed, dve_freed = sem("bank_full"), sem("act_freed"), sem("dve_freed")
        relu_read = sem("relu_read")
        scored, exp_done, prob_ready = sem("scored"), sem("exp_done"), sem("prob_ready")
        decay_ready, inner_ready = sem("decay_ready"), sem("inner_ready")
        ret_ssq, ret_root, ret_ready = sem("ret_ssq"), sem("ret_root"), sem("ret_ready")
        x2_done = sem("x2_done")
        logits_done, logits_read = sem("logits_done"), sem("logits_read")
        g_max, g_expd, e_max, e_expd = sem("g_max"), sem("g_expd"), sem("e_max"), sem("e_expd")
        sel_ready, ranks_done, flag_ready = sem("sel_ready"), sem("ranks_done"), sem("flag_ready")
        pick_ready, gather_done, h_e_ready = sem("pick_ready"), sem("gather_done"), sem("h_e_ready")
        gate_ready, gate_turned, gate_T_ready = sem("gate_ready"), sem("gate_turned"), sem("gate_T_ready")
        e_done, silu_step, hm_ready, hm_turned, hm_T_ready = (
            sem("e_done"), sem("silu_step"), sem("hm_ready"), sem("hm_turned"), sem("hm_T_ready"))
        y_ready, scattered, added = sem("y_ready"), sem("scattered"), sem("added")
        pick_step, pick_raw = sem("pick_step"), sem("pick_raw")
        dve_order, act_order, pool_order = sem("dve_order"), sem("act_order"), sem("pool_order")

        units = [(th, pair) for th in range(TH) for pair in range(HEADS // 2)]

        def s(*us):
            return [("s", u, "dve") for u in us]

        def a(kind, *what):
            return [(kind, w, "act") for w in what]

        uses = a("ik", 0) + a("iq", 0, 1, 2, 3)
        uses += a("dots", *[(0, jj, par) for jj in range(2) for par in range(2)])
        uses += a("dots", *[(1, jj, par) for jj in range(4) for par in range(2)])
        uses += a("ak", 0) + a("aq", 0, 1, 2, 3) + s(0, 1) + a("pt", 0, 1) + s(2, 3)
        uses += a("o", 0, 1) + a("pt", 2, 3) + a("o", 2, 3) + s(4, 5) + a("pt", 4, 5) + s(6, 7)
        uses += a("o", 4, 5) + a("pt", 6, 7) + a("o", 6, 7)
        uses += a("rq", 0, 1, 2, 3) + a("rk", 0, 1, 2, 3)
        uses += [("rs", hh, "inner") for hh in range(HEADS)] + a("ro", 0, 1, 2, 3) + a("rt", 0, 1, 2, 3)
        number = {(kind, what): n for n, (kind, what, _) in enumerate(uses)}

        def freed(n):
            who = uses[n][2]
            signal = {"act": act_freed, "dve": dve_freed, "inner": inner_ready}[who]
            return signal, sum(1 for w in uses[:n + 1] if w[2] == who)

        def bank(kind, what):
            return ps[:, 4 + number[(kind, what)] % 4, :]

        def zT_part(k):
            return zT[:, k % 4 * 4:k % 4 * 4 + 4, k // 4 * P:(k // 4 + 1) * P]

        def block_cols(pos):
            col = ORDER[pos] * BW
            return col, min(BW, IN_WIDTH - col)

        def unit(u):
            pos, e = u // BLOCK_UNITS, u % BLOCK_UNITS
            return pos, (2 * e, 2 * e + 1), block_cols(pos)[1]

        def split(buf, u):
            return buf[:, (u % SPLIT) * 1024:(u % SPLIT) * 1024 + 2 * unit(u)[2]]

        def raw(u):
            n = 2 * unit(u)[2]
            return ring[:, 8 + u // 2 % RAW, (u % 2) * n:(u % 2 + 1) * n]

        def width(th):
            return (th + 1) * P

        block = ctx.enter_context(nc.Block())

        @block.sync
        def _(sp):
            sp.dma_start(xs[:, 0, :], x_v[0]).then_inc(x_in[0], 16)
            sp.dma_start(xs[:, 1, :], x_v[1]).then_inc(x_in[1], 16)

            for q in range(UNITS // 2):
                if q >= RAW:
                    sp.wait_ge(lo_done, 2 * (q - RAW) + 2)
                at = ring[:, 8 + q % RAW, :]
                cq = q % 4
                col, n = block_cols(q // 4)
                sp.dma_start(at[:, 0:4 * n].rearrange("p (c n) -> p c n", c=4),
                             w_in_v[:, 4 * cq:4 * cq + 4, col:col + n]).then_inc(raw_landed[q % RAW], 16)

            def load(k, dst, src, wait):
                if wait is not None:
                    sp.wait_ge(ring_used, wait)
                sp.dma_start(dst, src).then_inc(landed[chunk_slot(k)], 16)

            for k in range(C):
                slot = chunk_slot(k)
                if k < 4:
                    sp.wait_ge(lo_done, UNITS - 6 + 2 * k)
                elif k == 4:
                    sp.wait_ge(unit_used, UNITS)
                nh, c = k // 8, k % 8 * 2
                load(k, ring[:, slot, :].rearrange("p (c n) -> p c n", c=2),
                     w_out_v[:, c:c + 2, nh * 1024:(nh + 1) * 1024], k - RING + 1 if k >= RING else None)

            def pair(it, number):
                for n in range(PAIR_CHUNKS):
                    k = MOE_CHUNK + n
                    if n < 16:
                        q, m = n // 4, n % 4
                        src = (w1_v if m < 2 else w3_v)[bass.ds(number * 2 + m % 2, 1), :, q * 2048:(q + 1) * 2048]
                    else:
                        q, m = (n - 16) // 2, n % 2
                        src = w2_v[bass.ds(number * 2 + m, 1), :, q * 2048:(q + 1) * 2048]
                    load(k, ring[:, chunk_slot(k), :], src.rearrange("o p n -> (o p) n"),
                         it * PAIR_CHUNKS + (k - RING + 1))

            def store(base):
                for i in range(4):
                    sp.wait_ge(added, base + 2 * i + 2)
                    th, cols = i // 2, slice(i % 2 * 1024, (i % 2 + 1) * 1024)
                    sp.dma_start(out_v[th][:, cols], xs[:, th, cols]).then_inc(stored, 16)

            with sp.Fori(0, PAIRS) as it:
                pair(it, it)
            sp.wait_ge(flag_ready, 1)
            over = sp.value_load(flag[0:1, 0:1], min_val=0, max_val=1)
            with sp.If(over > 0):
                with sp.Fori(1, PASSES) as pass_:
                    with sp.Fori(0, PAIRS) as number:
                        pair(pass_ * PAIRS + number, number)
                store(8 * (PASSES * PAIRS + 1))
            with sp.Else():
                store(8 * (PAIRS + 1))
            sp.wait_ge(stored, 16 * 4)

        @block.gpsimd
        def _(pool):
            pool.dma_start(g_row, norm1_g.partition_broadcast(P).rearrange("p l n -> p (l n)")).then_inc(g1_in, 16)
            pool.dma_start(const[:, :], consts).then_inc(const_in, 16)
            pool.wait_ge(z_turned, 8)
            for dst, src in ((gain_q, q_norm_g), (gain_k, k_norm_g), (ln_w, idx_k_ln_w), (ln_b, idx_k_ln_b)):
                pool.dma_start(dst, src.partition_broadcast(P).rearrange("p l n -> p (l n)")).then_inc(gains_in, 16)
            pool.wait_ge(gains_in, 64)
            for th in range(TH):
                pool.wait_ge(qk_scaled, th + 1)
                a_q = proj[:, th, AQ:AK].rearrange("p (h d) -> p h d", d=HD)
                a_k = proj[:, th, AK:AV].rearrange("p (h d) -> p h d", d=HD)
                pool.tensor_tensor(a_q, a_q, gain_q.unsqueeze(1).broadcast_to([P, HEADS, HD]), ALU.mult)
                pool.tensor_tensor(a_k, a_k, gain_k.unsqueeze(1).broadcast_to([P, KV, HD]), ALU.mult).then_inc(qk_done, 1)
            n = 0
            pool.wait_ge(const_in, 16)
            for part, blocks in ((RQ, 8), (RK, 10)):
                pool.wait_ge(evacuated, 2 * blocks)
                for th in range(TH):
                    v = proj[:, th, part:part + 1024].rearrange("p (h a d) -> p h a d", h=HEADS, a=2)
                    cos = const[:, COS + th * 64:COS + th * 64 + 64].unsqueeze(1).broadcast_to([P, HEADS, 64])
                    sin = const[:, SIN + th * 64:SIN + th * 64 + 64].unsqueeze(1).broadcast_to([P, HEADS, 64])
                    pool.tensor_tensor(rot[:, 0], v[:, :, 0, :], cos, ALU.mult)
                    pool.tensor_tensor(rot[:, 1], v[:, :, 1, :], sin, ALU.mult)
                    pool.tensor_tensor(rot[:, 2], v[:, :, 0, :], sin, ALU.mult)
                    pool.tensor_tensor(rot[:, 3], v[:, :, 1, :], cos, ALU.mult).then_inc(pool_order, 1)
                    n += 1
                    pool.wait_ge(pool_order, n)
                    pool.tensor_tensor(v[:, :, 0, :], rot[:, 0], rot[:, 1], ALU.subtract)
                    pool.tensor_tensor(v[:, :, 1, :], rot[:, 2], rot[:, 3], ALU.add).then_inc(rotated, 1)
                    pool.wait_ge(rotated, n)
            pool.wait_ge(bank_full, number[("o", 7)] + 1)
            pool.dma_start(gain_r, ret_norm_g.partition_broadcast(P).rearrange("p l n -> p (l n)")).then_inc(ret_gain_in, 16)
            pool.wait_ge(ret_ready, 1)
            pool.dma_start(g2_row, norm2_g.partition_broadcast(P).rearrange("p l n -> p (l n)")).then_inc(g2_in, 16)
            pool.dma_start(stage_g, w_group.rearrange("l (p c) g -> (l p) c g", c=C)).then_inc(router_in, 16)
            for g in range(GROUPS):
                pool.dma_start(stage_r[:, g], w_router[0, g].rearrange("(p c) e -> p c e", c=C)).then_inc(router_in, 16)
            pool.wait_ge(logits_done, 1)
            pool.memset(y_sb, 0.0).then_inc(y_ready, 4)
            pool.memset(gate_T, 0.0).then_inc(gate_T_ready, 1)

        @block.scalar
        def _(act):
            def norm_root(dst, src, n, signal):
                nc.scalar.activation(dst, src, ACT.Sqrt, bias=st[:, EPS_AT:EPS_AT + 1], scale=1.0 / n).then_inc(signal, 1)

            act.wait_ge(eps_set, 1)
            for th in range(TH):
                act.wait_ge(x_in[th], 16)
                nc.scalar.activation(buf_b[:, th * D:(th + 1) * D], xs[:, th, :], ACT.Square,
                                     accum_out=st[:, SSQ + th:SSQ + th + 1]).then_inc(ssq_done, 1)
            act.wait_ge(ssq_done, TH)
            norm_root(st[:, RSTD:RSTD + TH], st[:, SSQ:SSQ + TH], D, root_done)
            for k in range(8):
                act.wait_ge(z_turned, k + 1)
                nc.scalar.copy(zT_hi[:, k * 512:(k + 1) * 512], ps[:, k, :]).then_inc(zT_hi_done, 1)

            def round_unit(u):
                act.wait_ge(raw_landed[u // 2 % RAW], 16 * (u // 2 // RAW + 1))
                if u >= SPLIT:
                    act.wait_ge(unit_used, u - SPLIT + 1)
                nc.scalar.copy(split(w_hi, u), raw(u)).then_inc(hi_done, 1)

            def evacuate(pos):
                col, n = block_cols(pos)
                act.wait_ge(unit_used, BLOCK_UNITS * (pos + 1))
                for th in range(TH):
                    nc.scalar.activation(proj[:, th, col:col + n], ps[:, 2 * (pos % 2) + th, 0:n], ACT.Copy,
                                         scale=st[:, RSTD + th:RSTD + th + 1]).then_inc(evacuated, 1)

            def take(kind, what, dst, extra=None, func=None):
                act.wait_ge(bank_full, number[(kind, what)] + 1)
                if extra is not None:
                    act.wait_ge(*extra)
                src = bank(kind, what)
                src = src[:, 0:dst.shape[-1]] if len(dst.shape) == 2 else src
                if func is None:
                    nc.scalar.copy(dst, src).then_inc(act_freed, 1)
                else:
                    nc.scalar.activation(dst, src, func).then_inc(act_freed, 1)

            def flat2(ap):
                return ap.rearrange("p c t -> p (c t)")

            dots = [(th, jj, par) for th, jn in ((0, 2), (1, 4)) for jj in range(jn) for par in range(2)]

            def relus(*ns):
                for n in ns:
                    take("dots", dots[n], relu[:, n % 4, :], (relu_read, n - 3) if n >= 4 else None, ACT.Relu)

            def exps(*us):
                for u in us:
                    th = units[u][0]
                    act.wait_ge(scored, u + 1)
                    for b in range(2):
                        p_u = prob[:, u % 4, b, 0:width(th)]
                        last = nc.scalar.activation(p_u, p_u, ACT.Exp, bias=st[:, NEG + 2 * u + b:NEG + 2 * u + b + 1],
                                                    accum_out=st[:, SUM + 2 * u + b:SUM + 2 * u + b + 1])
                    last.then_inc(exp_done, 1)

            def take_pt(*us):
                for u in us:
                    if u >= 2:
                        act.wait_ge(bank_full, number[("o", u - 2)] + 1)
                    take("pt", u, p_t[:, u % 2, 0:2 * width(units[u][0])])

            def take_o(*us):
                for u in us:
                    th, pr = units[u]
                    act.wait_ge(bank_full, number[("o", u)] + 1)
                    nc.scalar.copy(mixedT(2 * pr, 2).rearrange("p (h t) -> p h t", h=2)[:, :, th * P:(th + 1) * P],
                                   bank("o", u)[:, 0:2 * P].rearrange("p (h t) -> p h t", h=2)).then_inc(act_freed, 1)

            def decays(*hs):
                for hh in hs:
                    if hh >= 4:
                        act.wait_ge(inner_ready, hh - 3)
                    nc.scalar.activation(decay[:, hh % 4, :], const[:, REL:REL + 256], ACT.Exp,
                                         scale=LOG_GAMMA[hh]).then_inc(decay_ready, 1)

            act.wait_ge(rstd_ready, 1)
            for u in range(UNITS):
                round_unit(u)
                if u % BLOCK_UNITS == 3 and u >= BLOCK_UNITS + 3:
                    evacuate(u // BLOCK_UNITS - 1)
                if u == 29:
                    act.wait_ge(ik_var, 1)
                    norm_root(st[:, VAR:VAR + 2], st[:, MU + 2:MU + 4], ID, ik_root)
                if u == 32:
                    take("ik", 0, ikT)
                    for k in range(3):
                        take("iq", k, flat2(iqT[:, 2 * k:2 * k + 2, :]))
                if u == 35:
                    take("iq", 3, flat2(iqT[:, 6:8, :]))
                    relus(0, 1)
                if u == 38:
                    relus(2, 3, 4, 5)
                if u == 41:
                    relus(6, 7, 8, 9)
                if u == 44:
                    relus(10, 11)
                if u in (51, 52):
                    act.wait_ge(evacuated, 12)
                    act.wait_ge(ik_var, 1)
                    nc.scalar.activation(sq[:, u - 51, :], proj[:, u - 51, AQ:AV], ACT.Square).then_inc(qk_squared, 1)
                if u == 57:
                    act.wait_ge(qk_ssq, 2)
                    norm_root(st[:, QKR:QKR + 20], st[:, QKS:QKS + 20], HD, qk_root)
                if u == 62:
                    take("ak", 0, flat2(akT))
                    for k in range(3):
                        take("aq", k, flat2(aqT[:, 2 * k:2 * k + 2, :]), (relu_read, 12))
                if u == 65:
                    take("aq", 3, flat2(aqT[:, 6:8, :]))
                    exps(0, 1)
                if u == 68:
                    take_pt(0, 1)
                    exps(2, 3)
                if u == 71:
                    take_o(0, 1)
                    take_pt(2, 3)
                if u == 74:
                    take_o(2, 3)
                    exps(4, 5)
                if u == 77:
                    take_pt(4, 5)
                    exps(6, 7)
                if u == 80:
                    take_o(4, 5)
                    take_pt(6, 7)
                if u == 83:
                    take_o(6, 7)
                if u == 88:
                    for k in range(4):
                        take("rq", k, flat2(rqT[:, 2 * k:2 * k + 2, :]))
                if u == 97:
                    for k in range(4):
                        take("rk", k, flat2(rkT[:, 2 * k:2 * k + 2, :]))
                    decays(0, 1, 2, 3)
                if u == 101:
                    decays(4, 5, 6, 7)
                if u == 108:
                    for k in range(4):
                        act.wait_ge(bank_full, number[("ro", k)] + 1)
                        col = RQ + 2 * k * HD
                        nc.scalar.copy(proj[:, :, col:col + 2 * HD].rearrange("p t (h d) -> p h t d", h=2),
                                       bank("ro", k).rearrange("p (h t d) -> p h t d", h=2, t=2)).then_inc(act_freed, 1)
            evacuate(BLOCKS - 1)
            act.wait_ge(evacuated, TH * BLOCKS)
            for th in range(TH):
                nc.scalar.activation(exp_g[:, th, :], proj[:, th, RG:RG + 1024], ACT.Exp, scale=-1.0).then_inc(silu_exp, 1)
            act.wait_ge(ret_ssq, 1)
            norm_root(st[:, RETR:RETR + 16], st[:, RETS:RETS + 16], HD, ret_root)
            for k in range(4):
                take("rt", k, mixedT(HEADS + 2 * k, 2))

            for i in range(4):
                nh, th = i // 2, i % 2
                act.wait_ge(x2_done, 2 * i + 2)
                nc.scalar.activation(buf_b[:, i * 1024:(i + 1) * 1024], xs[:, th, nh * 1024:(nh + 1) * 1024], ACT.Square,
                                     accum_out=st[:, SSQ2 + i:SSQ2 + i + 1]).then_inc(ssq_done, 1)
            act.wait_ge(rstd_ready, 2)
            norm_root(st[:, RSTD2:RSTD2 + TH], st[:, SSQ2:SSQ2 + TH], D, root_done)
            for k in range(0, 8, 2):
                act.wait_ge(z_turned, 8 + k + 1)
                nc.scalar.copy(zT_part(k), ps[:, k, :].rearrange("p (c t) -> p c t", c=4)).then_inc(zT_by_act, 1)
            for th in range(TH):
                act.wait_ge(g_max, th + 1)
                nc.scalar.activation(g_exp[:, th, :], logit[:, th, 0:GROUPS], ACT.Exp, bias=small[:, th, 0:1],
                                     accum_out=small[:, th, 1:2]).then_inc(g_expd, 1)
            for th in range(TH):
                act.wait_ge(e_max, th + 1)
                nc.scalar.activation(small[:, th, 3:4], top8[:, th, 1, 1:2], ACT.Exp,
                                     bias=small[:, th, 2:3]).then_inc(e_expd, 1)

            def gathered(g):
                for j in range(4):
                    act.wait_ge(gather_done, g * 4 + (j + 1))
                    nc.scalar.copy(h_e[:, 4 * j:4 * j + 4, :].rearrange("p c s -> p (c s)"),
                                   ps[:, 2 + j % 2, :]).then_inc(h_e_ready, 1)

            act.wait_ge(ring_used, C)
            gathered(0)

            def pair(it, more=True):
                act.wait_ge(ring_used, it * PAIR_CHUNKS + (MOE_CHUNK + 16))
                nc.scalar.activation(e_sb, ps[:, 0, :], ACT.Exp, scale=-1.0).then_inc(e_done, 1)
                if more:
                    gathered(it + 1)
                act.wait_ge(hm_turned, it + 1)
                nc.scalar.copy(hm_T.rearrange("p j s -> p (j s)"), ps[:, 2, :]).then_inc(hm_T_ready, 1)
                act.wait_ge(gate_turned, it + 2)
                nc.scalar.copy(gate_T, ps[:, 3, 0:2 * P]).then_inc(gate_T_ready, 1)
                act.wait_ge(ring_used, it * PAIR_CHUNKS + (MOE_CHUNK + PAIR_CHUNKS))
                for n in range(4):
                    nc.scalar.copy(y_sb[:, n * NB:(n + 1) * NB], ps[:, 4 + n, :]).then_inc(y_ready, 1)

            with act.Fori(0, PAIRS - 1) as it:
                pair(it)
            pair(PAIRS - 1, more=False)
            act.wait_ge(flag_ready, 1)
            over = act.value_load(flag[0:1, 0:1], min_val=0, max_val=1)
            with act.If(over > 0):
                gathered(PAIRS)
                with act.Fori(PAIRS, PASSES * PAIRS - 1) as it:
                    pair(it)
                pair(PASSES * PAIRS - 1, more=False)

        @block.vector
        def _(v):
            order = [0]

            def ordered(ins):
                order[0] += 1
                ins.then_inc(dve_order, 1)
                v.wait_ge(dve_order, order[0])

            V = nc.vector

            V.memset(st[:, EPS_AT:EPS_AT + 1], EPS).then_inc(eps_set, 1)

            def gained(g, th, q0, q1):
                V.tensor_tensor(z[:, th, :].rearrange("p (c q) -> p c q", c=C)[:, :, q0:q1],
                                xs[:, th, 16 * q0:16 * q1].rearrange("p (q c) -> p c q", c=C),
                                g[:, 16 * q0:16 * q1].rearrange("p (q c) -> p c q", c=C), ALU.mult).then_inc(z_done, 1)

            v.wait_ge(g1_in, 16)
            for th in range(TH):
                v.wait_ge(x_in[th], 16)
                gained(g_row, th, 0, P)
            v.wait_ge(root_done, 1)
            V.reciprocal(st[:, RSTD:RSTD + TH], st[:, RSTD:RSTD + TH]).then_inc(rstd_ready, 1)
            for k in range(8):
                v.wait_ge(zT_hi_done, k + 1)
                V.tensor_tensor(zT_lo[:, k * 512:(k + 1) * 512], ps[:, k, :],
                                zT_hi[:, k * 512:(k + 1) * 512].bitcast(F32), ALU.subtract).then_inc(zT_lo_done, 1)

            def rest_unit(u):
                v.wait_ge(hi_done, u + 1)
                V.tensor_tensor(split(w_lo, u), raw(u), split(w_hi, u).bitcast(F32), ALU.subtract).then_inc(lo_done, 1)

            ik = proj[:, :, IK:IK + ID]
            iw = proj[:, :, IW:IW + IH]
            heads = HEADS + KV

            def centre_ik():
                v.wait_ge(evacuated, 6)
                ordered(V.tensor_reduce(st[:, MU:MU + 2], ik, AX, ALU.add))
                ordered(V.tensor_scalar(st[:, MU:MU + 2], st[:, MU:MU + 2], 1.0 / ID, None, ALU.mult))
                ordered(V.tensor_tensor(ik, ik, st[:, MU:MU + 2].unsqueeze(2).broadcast_to([P, TH, ID]), ALU.subtract))
                sq_i = sq[:, 0, 0:TH * ID].rearrange("p (t d) -> p t d", t=TH)
                ordered(V.tensor_tensor(sq_i, ik, ik, ALU.mult))
                V.tensor_reduce(st[:, MU + 2:MU + 4], sq_i, AX, ALU.add).then_inc(ik_var, 1)
                v.wait_ge(ik_var, 1)
                ordered(V.tensor_scalar(iw, iw, IH ** -0.5 * ID ** -0.5, None, ALU.mult))

            def finish_ik():
                v.wait_ge(ik_root, 1)
                v.wait_ge(gains_in, 64)
                ordered(V.reciprocal(st[:, VAR:VAR + 2], st[:, VAR:VAR + 2]))
                for th in range(TH):
                    ordered(V.scalar_tensor_tensor(ik[:, th], ik[:, th], st[:, VAR + th:VAR + th + 1], ln_w,
                                                   ALU.mult, ALU.mult))
                    V.tensor_tensor(ik_dup[:, th, 0:ID], ik[:, th], ln_b, ALU.add)
                    V.tensor_tensor(ik_dup[:, th, ID:2 * ID], ik[:, th], ln_b, ALU.add).then_inc(index_ready, 1)
                ordered(V.memset(score, 0.0))

            def qk_squares(th):
                v.wait_ge(qk_squared, th + 1)
                V.tensor_reduce(st[:, QKS + heads * th:QKS + heads * (th + 1)],
                                sq[:, th, :].rearrange("p (h d) -> p h d", d=HD), AX, ALU.add).then_inc(qk_ssq, 1)

            def qk_scale(th):
                if th == 0:
                    v.wait_ge(qk_root, 1)
                    ordered(V.reciprocal(st[:, QKR:QKR + 20], st[:, QKR:QKR + 20]))
                part = proj[:, th, AQ:AV].rearrange("p (h d) -> p h d", d=HD)
                r = st[:, QKR + heads * th:QKR + heads * (th + 1)]
                V.tensor_tensor(part, part, r.unsqueeze(2).broadcast_to([P, heads, HD]), ALU.mult).then_inc(qk_scaled, 1)

            dots = [(th, jj, par) for th, jn in ((0, 2), (1, 4)) for jj in range(jn) for par in range(2)]

            def index_scores(*ns):
                for n in ns:
                    th, jj, par = dots[n]
                    w, per = width(th), NB // width(th)
                    v.wait_ge(act_freed, freed(number[("dots", dots[n])])[1])
                    for i in range(per):
                        head = 2 * (per * jj + i) + par
                        ins = V.scalar_tensor_tensor(score[:, th, 0:w], relu[:, n % 4, i * w:(i + 1) * w],
                                                     proj[:, th, IW + head:IW + head + 1], score[:, th, 0:w],
                                                     ALU.mult, ALU.add)
                        if i < per - 1:
                            ordered(ins)
                    ins.then_inc(relu_read, 1)
                    v.wait_ge(relu_read, n + 1)

            def hide():
                for th in range(TH):
                    w = width(th)
                    last = V.memset(score[0:CHUNK, th, w - CHUNK:w], HIDDEN)
                ordered(last)

            def choose(rounds):
                for _ in range(rounds):
                    for th in range(TH):
                        last = V.max(st[:, M8 + 8 * th:M8 + 8 * th + 8], score[:, th, 0:width(th)])
                    ordered(last)
                    for th in range(TH):
                        sc = score[:, th, 0:width(th)]
                        last = V.match_replace(sc, st[:, M8 + 8 * th:M8 + 8 * th + 8], sc, SENT)
                    ordered(last)

            def mask():
                for th in range(TH):
                    w = width(th)
                    last = V.tensor_scalar(bias[:, th, 0:w], score[:, th, 0:w], SENT, OFF, ALU.is_gt, ALU.mult)
                ordered(last)

            def scores(*us):
                for u in us:
                    th = units[u][0]
                    w = width(th)
                    v.wait_ge(bank_full, number[("s", u)] + 1)
                    if u >= 4:
                        v.wait_ge(bank_full, number[("pt", u - 4)] + 1)
                    p_u = prob[:, u % 4, :, 0:w]
                    V.scalar_tensor_tensor(p_u, bank("s", u).rearrange("p (h s) -> p h s", h=2)[:, :, 0:w], HD ** -0.5,
                                           bias[:, th, 0:w].unsqueeze(1).broadcast_to([P, 2, w]),
                                           ALU.mult, ALU.add).then_inc(dve_freed, 1)
                    v.wait_ge(dve_freed, freed(number[("s", u)])[1])
                    m = st[:, NEG + 2 * u:NEG + 2 * u + 2]
                    ordered(V.tensor_reduce(m, p_u, AX, ALU.max))
                    V.tensor_scalar(m, m, -1.0, None, ALU.mult).then_inc(scored, 1)

            def probs(*us):
                for u in us:
                    w = width(units[u][0])
                    v.wait_ge(exp_done, u + 1)
                    r = st[:, RCP + 2 * u:RCP + 2 * u + 2]
                    ordered(V.reciprocal(r, st[:, SUM + 2 * u:SUM + 2 * u + 2]))
                    p_u = prob[:, u % 4, :, 0:w]
                    V.tensor_tensor(p_u, p_u, r.unsqueeze(2).broadcast_to([P, 2, w]), ALU.mult).then_inc(prob_ready, 1)

            def inners(*hs):
                for hh in hs:
                    v.wait_ge(decay_ready, hh + 1)
                    v.wait_ge(bank_full, number[("rs", hh)] + 1)
                    b = bank("rs", hh)
                    V.scalar_tensor_tensor(inner[:, hh, 0:256], b[:, 0:256], HD ** -0.5, decay[:, hh % 4, 0:256],
                                           ALU.mult, ALU.mult)
                    V.scalar_tensor_tensor(inner[:, hh, 256:384], b[:, 256:384], HD ** -0.5,
                                           decay[:, hh % 4, 0:128], ALU.mult, ALU.mult).then_inc(inner_ready, 1)

            for u in range(UNITS):
                rest_unit(u)
                if u == 28:
                    centre_ik()
                if u == 30:
                    finish_ik()
                if u == 36:
                    index_scores(0, 1)
                if u == 39:
                    index_scores(2, 3, 4, 5)
                if u == 42:
                    index_scores(6, 7, 8, 9)
                if u == 45:
                    index_scores(10, 11)
                    hide()
                if 46 <= u < 46 + TOPK // 8:
                    choose(1)
                if u == 46 + TOPK // 8:
                    mask()
                if u in (55, 56):
                    qk_squares(u - 55)
                if u in (58, 59):
                    qk_scale(u - 58)
                if u == 65:
                    scores(0, 1)
                if u == 66:
                    probs(0, 1)
                if u == 68:
                    scores(2, 3)
                if u == 69:
                    probs(2, 3)
                if u == 74:
                    scores(4, 5)
                if u == 75:
                    probs(4, 5)
                if u == 77:
                    scores(6, 7)
                if u == 78:
                    probs(6, 7)
                if u == 100:
                    inners(0, 1, 2, 3)
                if u == 103:
                    inners(4, 5, 6, 7)
            ret = proj[:, :, RQ:RQ + 1024]
            rg = proj[:, :, RG:RG + 1024]
            v.wait_ge(act_freed, freed(number[("ro", 3)])[1])
            ordered(V.tensor_tensor(sq_r, ret, ret, ALU.mult))
            V.tensor_reduce(st[:, RETS:RETS + 16], sq_r.rearrange("p t (h d) -> p (t h) d", d=HD), AX,
                            ALU.add).then_inc(ret_ssq, 1)
            v.wait_ge(ret_gain_in, 16)
            ordered(V.tensor_tensor(ret, ret, gain_r.unsqueeze(1).broadcast_to([P, TH, 1024]), ALU.mult))
            v.wait_ge(silu_exp, 2)
            ordered(V.tensor_scalar(exp_g, exp_g, 1.0, None, ALU.add))
            ordered(V.reciprocal(exp_g, exp_g))
            V.tensor_tensor(rg, rg, exp_g, ALU.mult)
            v.wait_ge(ret_root, 1)
            ordered(V.reciprocal(st[:, RETR:RETR + 16], st[:, RETR:RETR + 16]))
            for th in range(TH):
                r4 = ret[:, th].rearrange("p (h d) -> p h d", d=HD)
                last = V.tensor_tensor(r4, r4, st[:, RETR + 8 * th:RETR + 8 * th + 8].unsqueeze(2).broadcast_to([P, HEADS, HD]),
                                       ALU.mult)
            ordered(last)
            V.tensor_tensor(ret, ret, rg, ALU.mult).then_inc(ret_ready, 1)

            def second_half(nh):
                v.wait_ge(ring_used, 8 * (nh + 1))
                for th in range(TH):
                    for n in range(2):
                        i = nh * 4 + th * 2 + n
                        xo = xs[:, th, nh * 1024 + n * NB:nh * 1024 + (n + 1) * NB]
                        V.tensor_tensor(xo, xo, ps[:, i, :], ALU.add).then_inc(x2_done, 1)
                    v.wait_ge(x2_done, nh * 4 + th * 2 + 2)
                    if nh == 0 and th == 0:
                        v.wait_ge(g2_in, 16)
                    gained(g2_row, th, nh * 64, nh * 64 + 64)

            second_half(0)
            v.wait_ge(router_in, 80)
            V.tensor_copy(gates_w[:, :, 0:GROUPS], stage_g)
            for g in range(GROUPS):
                last = V.tensor_copy(gates_w[:, :, GROUPS + g * 8:GROUPS + g * 8 + 8], stage_r[:, g])
            ordered(last)
            ordered(V.memset(g_pad[:], OFF))
            second_half(1)
            v.wait_ge(ssq_done, TH + 4)
            V.tensor_tensor(st[:, SSQ2:SSQ2 + TH], st[:, SSQ2:SSQ2 + TH], st[:, SSQ2 + TH:SSQ2 + 2 * TH],
                            ALU.add).then_inc(rstd_ready, 1)
            v.wait_ge(root_done, 2)
            ordered(V.reciprocal(st[:, RSTD2:RSTD2 + TH], st[:, RSTD2:RSTD2 + TH]))
            for k in range(1, 8, 2):
                v.wait_ge(z_turned, 8 + k + 1)
                V.tensor_copy(zT_part(k), ps[:, k, :].rearrange("p (c t) -> p c t", c=4)).then_inc(zT_by_dve, 1)

            v.wait_ge(logits_done, 1)
            for th in range(TH):
                last = V.tensor_scalar(logit[:, th, :], ps[:, 0, th * 36:th * 36 + 36], st[:, RSTD2 + th:RSTD2 + th + 1],
                                       None, ALU.mult)
            ordered(last)
            ordered(V.tensor_copy(g_pad[:, :, 0:GROUPS], logit[:, :, 0:GROUPS]))
            for th in range(TH):
                ordered(V.max(top8[:, th, 0, :], g_pad[:, th, :]))
                V.tensor_scalar(small[:, th, 0:1], top8[:, th, 0, 0:1], -1.0, None, ALU.mult).then_inc(g_max, 1)
                ordered(V.max_index(idx8[:, th, 0, :], top8[:, th, 0, :], g_pad[:, th, :]))
            ordered(V.tensor_copy(idxf[:, :, 0, :], idx8[:, :, 0, :]))
            for th in range(TH):
                ordered(V.tensor_scalar(oh[:, th, 0, :], iota[:, 0:8], idxf[:, th, 0, 0:1], None, ALU.is_equal))
            for th in range(TH):
                last = V.tensor_tensor(pick[:, th], logit[:, th, GROUPS:36].rearrange("p (g n) -> p g n", g=GROUPS),
                                       oh[:, th, 0, 0:GROUPS].unsqueeze(2).broadcast_to([P, GROUPS, 8]), ALU.mult)
            ordered(last)
            for th in range(TH):
                last = V.tensor_reduce(e_sel[:, th], pick[:, th].rearrange("p g n -> p n g"), AX, ALU.add)
            ordered(last)
            for th in range(TH):
                ordered(V.max(top8[:, th, 1, :], e_sel[:, th]))
                V.tensor_scalar(small[:, th, 2:3], top8[:, th, 1, 0:1], -1.0, None, ALU.mult).then_inc(e_max, 1)
                ordered(V.max_index(idx8[:, th, 1, :], top8[:, th, 1, :], e_sel[:, th]))
            ordered(V.tensor_copy(idxf[:, :, 1, :], idx8[:, :, 1, :]))
            for th in range(TH):
                for a in range(2):
                    last = V.tensor_scalar(oh[:, th, 1 + a, :], iota[:, 0:8], idxf[:, th, 1, a:a + 1], None, ALU.is_equal)
            ordered(last)
            V.tensor_tensor(cs[:, :, 1, :], oh[:, :, 1, :], oh[:, :, 2, :], ALU.add)
            v.wait_ge(g_expd, 2)
            v.wait_ge(e_expd, 2)
            ordered(V.tensor_scalar(small[:, :, 4:5], small[:, :, 3:4], 1.0, None, ALU.add))
            ordered(V.tensor_tensor(small[:, :, 4:5], small[:, :, 4:5], small[:, :, 1:2], ALU.mult))
            ordered(V.reciprocal(small[:, :, 5:6], small[:, :, 4:5]))
            ordered(V.tensor_tensor(small[:, :, 6:7], small[:, :, 5:6], small[:, :, 3:4], ALU.mult))
            for th in range(TH):
                ordered(V.tensor_scalar(cs[:, th, 0, :], oh[:, th, 1, :], small[:, th, 5:6], None, ALU.mult))
                ordered(V.scalar_tensor_tensor(cs[:, th, 0, :], oh[:, th, 2, :], small[:, th, 6:7], cs[:, th, 0, :],
                                               ALU.mult, ALU.add))
                for dst, a in ((comb, 0), (sel, 1)):
                    last = V.tensor_tensor(dst[:, th].rearrange("p (g n) -> p g n", g=GROUPS),
                                           oh[:, th, 0, 0:GROUPS].unsqueeze(2).broadcast_to([P, GROUPS, 8]),
                                           cs[:, th, a, :].unsqueeze(1).broadcast_to([P, GROUPS, 8]), ALU.mult)
            last.then_inc(sel_ready, 1)
            v.wait_ge(sel_ready, 1)
            v.wait_ge(ranks_done, 1)
            ordered(V.tensor_scalar(posm, ps[:, 1, 0:64].rearrange("p (t e) -> p t e", t=TH), 1.0, None, ALU.add))
            ordered(V.tensor_tensor(posm, posm, sel, ALU.mult))
            ordered(V.tensor_scalar(posm, posm, -1.0, None, ALU.add))
            ordered(V.tensor_reduce(small[:, 0, 7:8], ps[:, 1, 64:96], AX, ALU.max))
            V.tensor_scalar(flag[:, :], small[:, 0, 7:8], float(SLOTS), None, ALU.is_gt).then_inc(flag_ready, 1)
            v.sem_inc(added, 8)
            v.sem_inc(gate_turned, 1)

            def slots(src, g):
                pass_, pr = (g >> 4) & (PASSES - 1), g & (PAIRS - 1)
                it = iota[:, bass.ds(pass_ * SLOTS, SLOTS)].unsqueeze(1).unsqueeze(1).broadcast_to([P, TH, 2, SLOTS])
                col = src[:, :, bass.ds(pr * 2, 2)].unsqueeze(3).broadcast_to([P, TH, 2, SLOTS])
                return it, col

            rstd2 = st[:, RSTD2:RSTD2 + TH].unsqueeze(2).unsqueeze(3).broadcast_to([P, TH, 2, SLOTS])

            def pick_tokens(g):
                it, col = slots(posm, g)
                V.tensor_tensor(pick_p, col, it, ALU.is_equal).then_inc(pick_raw, 1)
                v.wait_ge(pick_raw, g + 1)
                V.tensor_tensor(pick_p, pick_p, rstd2, ALU.mult).then_inc(pick_ready, 1)

            pick_tokens(0)

            def pair(it, more=True):
                v.wait_ge(gate_turned, it + 1)
                i, col = slots(posm, it)
                V.tensor_tensor(gate_p, col, i, ALU.is_equal).then_inc(pick_step, 1)
                v.wait_ge(pick_step, it + 1)
                V.tensor_tensor(gate_p, gate_p, slots(comb, it)[1], ALU.mult).then_inc(gate_ready, 1)
                v.wait_ge(gather_done, it * 4 + 4)
                if more:
                    pick_tokens(it + 1)
                add_scattered(it)
                v.wait_ge(e_done, it + 1)
                V.tensor_scalar(e_sb, e_sb, 1.0, None, ALU.add).then_inc(silu_step, 1)
                v.wait_ge(silu_step, it * 3 + 1)
                V.reciprocal(e_sb, e_sb).then_inc(silu_step, 1)
                v.wait_ge(silu_step, it * 3 + 2)
                V.tensor_tensor(e_sb, e_sb, ps[:, 0, :], ALU.mult).then_inc(silu_step, 1)
                v.wait_ge(silu_step, it * 3 + 3)
                V.tensor_tensor(hm.rearrange("p (j q) -> p j q", j=J), e_sb.rearrange("p (q j) -> p j q", j=J),
                                ps[:, 1, :].rearrange("p (q j) -> p j q", j=J), ALU.mult).then_inc(hm_ready, 1)

            def add_scattered(it):
                for s in range(8):
                    v.wait_ge(scattered, it * 8 + (s + 1))
                    th, n = s // 4, s % 4
                    xo = xs[:, th, n * NB:(n + 1) * NB]
                    V.tensor_tensor(xo, xo, ps[:, 3 - s % 2, :], ALU.add).then_inc(added, 1)

            with v.Fori(0, PAIRS - 1) as it:
                pair(it)
            pair(PAIRS - 1, more=False)
            v.wait_ge(flag_ready, 1)
            over = v.value_load(flag[0:1, 0:1], min_val=0, max_val=1)
            with v.If(over > 0):
                pick_tokens(PAIRS)
                with v.Fori(PAIRS, PASSES * PAIRS - 1) as it:
                    pair(it)
                pair(PASSES * PAIRS - 1, more=False)
                add_scattered(PASSES * PAIRS)
            with v.Else():
                add_scattered(PAIRS)

        @block.tensor
        def _(pe):
            mm = nc.tensor.matmul

            def turn_z():
                for k in range(8):
                    for cc in range(2):
                        for th in range(TH):
                            c = 2 * k + cc
                            last = nc.tensor.transpose(ps[:, k, (2 * cc + th) * P:(2 * cc + th + 1) * P],
                                                       z[:, th, c * P:(c + 1) * P], ident)
                    last.then_inc(z_turned, 1)

            pe.wait_ge(const_in, 16)
            pe.wait_ge(z_done, TH)
            turn_z()

            zh = zT_hi[:, :].rearrange("p (c t) -> p c t", c=C)
            zl = zT_lo[:, :].rearrange("p (c t) -> p c t", c=C)

            def project(u):
                pos, chunks, n = unit(u)
                if pos == 0:
                    pe.wait_ge(zT_lo_done, max(TH, u + 1))
                elif u % BLOCK_UNITS == 0:
                    if pos == 1:
                        pe.wait_ge(zT_lo_done, 4)
                    else:
                        pe.wait_ge(evacuated, TH * (pos - 1))
                pe.wait_ge(lo_done, u + 1)
                for i, c in enumerate(chunks):
                    wh = split(w_hi, u)[:, i * n:(i + 1) * n]
                    wl = split(w_lo, u)[:, i * n:(i + 1) * n]
                    for th in range(TH):
                        b = ps[:, 2 * (pos % 2) + th, 0:n]
                        t = slice(th * P, (th + 1) * P)
                        mm(b, zh[:, c, t], wh, start=(c == 0), stop=False)
                        mm(b, zh[:, c, t], wl, start=False, stop=False)
                        last = mm(b, zl[:, c, t], wh, start=False, stop=(c == C - 1))
                last.then_inc(unit_used, 1)

            def fill(kind, what):
                n = number[(kind, what)]
                if n >= 4:
                    pe.wait_ge(*freed(n - 4))
                return ps[:, 4 + n % 4, :]

            def turn(kind, what, pieces):
                b = fill(kind, what)
                for i, piece in enumerate(pieces):
                    last = nc.tensor.transpose(b[:, i * P:(i + 1) * P], piece, ident)
                last.then_inc(bank_full, 1)

            def head_pair(part, k):
                return [proj[:, th, part + hh * HD:part + (hh + 1) * HD] for hh in (2 * k, 2 * k + 1) for th in range(TH)]

            def dots(th, *jjs):
                w = width(th)
                per = NB // w
                for jj in jjs:
                    pe.wait_ge(*freed(number[("iq", (per * jj + per - 1) // 2)]))
                    banks = [fill("dots", (th, jj, par)) for par in range(2)]
                    for i in range(per):
                        for par in range(2):
                            rows = slice(ID * par, ID * par + ID)
                            last = mm(banks[par][:, i * w:(i + 1) * w], iqT[rows, per * jj + i, th * P:(th + 1) * P],
                                      ikT[rows, 0:w], start=True, stop=True)
                    last.then_inc(bank_full, 2)

            def scores(*us):
                for u in us:
                    th, pr = units[u]
                    pe.wait_ge(*freed(number[("aq", pr)]))
                    b = fill("s", u)
                    for k in range(2):
                        last = mm(b[:, k * 256:k * 256 + width(th)], aqT[:, 2 * pr + k, th * P:(th + 1) * P],
                                  akT[:, pr // 2, 0:width(th)], start=True, stop=True)
                    last.then_inc(bank_full, 1)

            def turn_probs(*us):
                for u in us:
                    th = units[u][0]
                    b = fill("pt", u)
                    pe.wait_ge(prob_ready, u + 1)
                    for k in range(2):
                        for sh in range(th + 1):
                            i = k * (th + 1) + sh
                            last = nc.tensor.transpose(b[:, i * P:(i + 1) * P], prob[:, u % 4, k, sh * P:(sh + 1) * P], ident)
                    last.then_inc(bank_full, 1)

            def attend(*us):
                for u in us:
                    th, pr = units[u]
                    b = fill("o", u)
                    pe.wait_ge(*freed(number[("pt", u)]))
                    for k in range(2):
                        for sh in range(th + 1):
                            i = k * (th + 1) + sh
                            last = mm(b[:, k * P:(k + 1) * P], proj[:, sh, AV + (pr // 2) * HD:AV + (pr // 2 + 1) * HD],
                                      p_t[:, u % 2, i * P:(i + 1) * P], start=(sh == 0), stop=(sh == th))
                    last.then_inc(bank_full, 1)

            def ret_scores(*hs):
                for hh in hs:
                    b = fill("rs", hh)
                    mm(b[:, 0:256], rkT[:, hh, 0:P], rqT[:, hh, :], start=True, stop=True)
                    mm(b[:, 256:384], rkT[:, hh, P:2 * P], rqT[:, hh, P:2 * P], start=True, stop=True).then_inc(bank_full, 1)

            def retain(*ks):
                for k in ks:
                    b = fill("ro", k)
                    pe.wait_ge(inner_ready, 2 * k + 2)
                    for i in range(2):
                        s_h = inner[:, 2 * k + i, :]
                        rv = [proj[:, th, RV + (2 * k + i) * HD:RV + (2 * k + i + 1) * HD] for th in range(TH)]
                        mm(b[:, i * 256:i * 256 + P], s_h[:, 0:P], rv[0], start=True, stop=True)
                        mm(b[:, i * 256 + P:i * 256 + 2 * P], s_h[:, P:2 * P], rv[0], start=True, stop=False)
                        last = mm(b[:, i * 256 + P:i * 256 + 2 * P], s_h[:, 2 * P:3 * P], rv[1], start=False, stop=True)
                    last.then_inc(bank_full, 1)

            for u in range(UNITS):
                project(u)
                if u == 30:
                    pe.wait_ge(index_ready, 2)
                    turn("ik", 0, [ik_dup[:, th, :] for th in range(TH)])
                    for k in range(3):
                        turn("iq", k, head_pair(IQ, k))
                if u == 33:
                    turn("iq", 3, head_pair(IQ, 3))
                    dots(0, 0)
                if u == 36:
                    dots(0, 1)
                    dots(1, 0)
                if u == 39:
                    dots(1, 1, 2)
                if u == 42:
                    dots(1, 3)
                if u == 60:
                    pe.wait_ge(qk_done, 2)
                    turn("ak", 0, head_pair(AK, 0))
                    for k in range(3):
                        turn("aq", k, head_pair(AQ, k))
                if u == 63:
                    turn("aq", 3, head_pair(AQ, 3))
                    scores(0, 1)
                if u == 66:
                    turn_probs(0, 1)
                    scores(2, 3)
                if u == 69:
                    attend(0, 1)
                    turn_probs(2, 3)
                if u == 72:
                    attend(2, 3)
                    scores(4, 5)
                if u == 75:
                    turn_probs(4, 5)
                    scores(6, 7)
                if u == 78:
                    attend(4, 5)
                    turn_probs(6, 7)
                if u == 81:
                    attend(6, 7)
                if u == 86:
                    pe.wait_ge(rotated, 2)
                    for k in range(4):
                        turn("rq", k, head_pair(RQ, k))
                if u == 95:
                    pe.wait_ge(rotated, 4)
                    for k in range(4):
                        turn("rk", k, head_pair(RK, k))
                if u == 98:
                    pe.wait_ge(*freed(number[("rk", 3)]))
                    ret_scores(0, 1, 2, 3)
                if u == 101:
                    ret_scores(4, 5, 6, 7)
                if u == 106:
                    retain(0, 1, 2, 3)

            pe.wait_ge(evacuated, TH * len(ORDER))
            for k in range(C):
                nh, cp = k // 8, k % 8
                if cp == 4 and nh == 0:
                    pe.wait_ge(ret_ready, 1)
                    for i in range(4):
                        turn("rt", i, head_pair(RQ, i))
                    pe.wait_ge(*freed(number[("rt", 3)]))
                slot = chunk_slot(k)
                pe.wait_ge(landed[slot], chunk_landed(k))
                for cc in range(2):
                    c = 2 * cp + cc
                    for th in range(TH):
                        for n in range(2):
                            last = mm(ps[:, 4 * nh + 2 * th + n, :], mixedT(c)[:, th * P:(th + 1) * P],
                                      ring[:, slot, cc * 1024 + n * NB:cc * 1024 + (n + 1) * NB],
                                      start=(c == 0), stop=(c == C - 1))
                last.then_inc(ring_used, 1)

            def turn_z2(k):
                th = k // 4
                for cc in range(4):
                    c = k % 4 * 4 + cc
                    last = nc.tensor.transpose(ps[:, k, cc * P:(cc + 1) * P], z[:, th, c * P:(c + 1) * P], ident)
                last.then_inc(z_turned, 1)

            def logits(k):
                th = k // 4
                pe.wait_ge(zT_by_act, k // 2 + 1)
                if k % 2:
                    pe.wait_ge(zT_by_dve, k // 2 + 1)
                for cc in range(4):
                    c = k % 4 * 4 + cc
                    last = mm(ps[:, 0, th * 36:th * 36 + 36], zT[:, c, th * P:(th + 1) * P], gates_w[:, c, :],
                              start=(c == 0), stop=(c == C - 1))
                return last

            pe.wait_ge(z_done, TH + 3)
            pe.wait_ge(x2_done, 8)
            for k in range(4):
                turn_z2(k)
            pe.wait_ge(z_done, TH + 4)
            for k in range(4, 8):
                turn_z2(k)
                logits(k - 4)
            for k in range(4, 8):
                last = logits(k)
            last.then_inc(logits_done, 1)
            pe.wait_ge(sel_ready, 1)
            mm(ps[:, 1, 0:32], before, sel[:, 0, :], start=True, stop=True)
            mm(ps[:, 1, 32:64], ones, sel[:, 0, :], start=True, stop=False)
            mm(ps[:, 1, 32:64], before, sel[:, 1, :], start=False, stop=True)
            mm(ps[:, 1, 64:96], ones, sel[:, 0, :], start=True, stop=False)
            mm(ps[:, 1, 64:96], ones, sel[:, 1, :], start=False, stop=True).then_inc(ranks_done, 1)

            def gather(g, waits):
                pe.wait_ge(pick_ready, g + 1)
                for j in range(4):
                    waits(j)
                    for c in range(4 * j, 4 * j + 4):
                        for th in range(TH):
                            last = mm(ps[:, 2 + j % 2, (c % 4) * P:(c % 4 + 1) * P], z[:, th, c * P:(c + 1) * P],
                                      pick_p[:, th].rearrange("p e s -> p (e s)"), start=(th == 0), stop=(th == TH - 1))
                    last.then_inc(gather_done, 1)

            def wait_copied(base):
                def waits(j):
                    if j >= 2:
                        pe.wait_ge(h_e_ready, base + (j - 1))
                return waits

            gather(0, wait_copied(0))

            def scatter(it):
                pe.wait_ge(y_ready, it * 4 + 4)
                pe.wait_ge(gate_T_ready, it + 1)
                for s in range(8):
                    if s >= 2:
                        pe.wait_ge(added, it * 8 + (8 + s - 1))
                    th, n = s // 4, s % 4
                    mm(ps[:, 3 - s % 2, :], gate_T[:, th * P:(th + 1) * P], y_sb[:, n * NB:(n + 1) * NB],
                       start=True, stop=True).then_inc(scattered, 1)

            def landed_now(it, n):
                k = MOE_CHUNK + n
                pe.wait_ge(landed[chunk_slot(k)], it * (16 * PAIR_CHUNKS // RING) + chunk_landed(k))
                return ring[:, chunk_slot(k), :]

            def pair(it, more=True):
                pe.wait_ge(h_e_ready, it * 4 + 4)
                for q in range(4):
                    w = [landed_now(it, 4 * q + m) for m in range(4)]
                    for cc in range(4):
                        c = 4 * q + cc
                        for m in range(4):
                            half = slice(SLOTS * (m % 2), SLOTS * (m % 2 + 1))
                            last = mm(ps[half, m // 2, :], h_e[:, c, half], w[m][:, cc * NB:(cc + 1) * NB],
                                      start=(c == 0), stop=(c == C - 1))
                    last.then_inc(ring_used, 4)
                    if q == 1:
                        scatter(it)

                def waits(j):
                    if j < 2:
                        pe.wait_ge(added, it * 8 + (16 - j))
                    else:
                        pe.wait_ge(h_e_ready, it * 4 + (4 + j - 1))
                if more:
                    gather(it + 1, waits)
                    pe.wait_ge(h_e_ready, it * 4 + 7)
                else:
                    pe.wait_ge(added, it * 8 + 16)
                pe.wait_ge(hm_ready, it + 1)
                for j in range(J):
                    last = nc.tensor.transpose(ps[:, 2, j * P:(j + 1) * P], hm[:, j * P:(j + 1) * P], ident)
                last.then_inc(hm_turned, 1)
                if more:
                    pe.wait_ge(h_e_ready, it * 4 + 8)
                pe.wait_ge(gate_ready, it + 1)
                for th in range(TH):
                    last = nc.tensor.transpose(ps[:, 3, th * P:(th + 1) * P],
                                               gate_p[:, th].rearrange("p e s -> p (e s)"), ident)
                last.then_inc(gate_turned, 1)
                pe.wait_ge(hm_T_ready, it + 1)
                for j in range(J):
                    w = [landed_now(it, 16 + 2 * j + m) for m in range(2)]
                    for n in range(4):
                        for m in range(2):
                            half = slice(SLOTS * m, SLOTS * (m + 1))
                            last = mm(ps[half, 4 + n, :], hm_T[:, j, half], w[m][:, n * NB:(n + 1) * NB],
                                      start=(j == 0), stop=(j == J - 1))
                    last.then_inc(ring_used, 2)

            with pe.Fori(0, PAIRS - 1) as it:
                pair(it)
            pair(PAIRS - 1, more=False)

            def last_scatter(it):
                pe.wait_ge(y_ready, it * 4 + 4)
                pe.wait_ge(gate_T_ready, it + 1)
                pe.wait_ge(added, it * 8 + 8)
                for s in range(8):
                    if s >= 2:
                        pe.wait_ge(added, it * 8 + (8 + s - 1))
                    th, n = s // 4, s % 4
                    mm(ps[:, 3 - s % 2, :], gate_T[:, th * P:(th + 1) * P], y_sb[:, n * NB:(n + 1) * NB],
                       start=True, stop=True).then_inc(scattered, 1)

            pe.wait_ge(flag_ready, 1)
            over = pe.value_load(flag[0:1, 0:1], min_val=0, max_val=1)
            with pe.If(over > 0):
                def waits(j):
                    if j == 0:
                        pe.wait_ge(added, PAIRS * 8 + 8)
                    elif j == 1:
                        pe.wait_ge(gate_T_ready, PAIRS + 1)
                    else:
                        pe.wait_ge(h_e_ready, PAIRS * 4 + (j - 1))
                gather(PAIRS, waits)
                with pe.Fori(PAIRS, PASSES * PAIRS - 1) as it:
                    pair(it)
                pair(PASSES * PAIRS - 1, more=False)
                last_scatter(PASSES * PAIRS)
            with pe.Else():
                last_scatter(PAIRS)


def constants():
    t = np.zeros((P, CONSTS), np.float32)
    p = np.arange(P)
    t[:, IDENT:IDENT + P] = np.eye(P)
    t[:, BEFORE:BEFORE + P] = p[:, None] < p[None, :]
    t[:, ONES:ONES + P] = 1.0
    inv = np.float32(1.0) / (np.float32(10000.0) ** np.linspace(0.0, 1.0, HD // 2, dtype=np.float32))
    ang = (np.arange(SEQ, dtype=np.float32)[:, None] * inv[None, :]).astype(np.float32)
    for th in range(TH):
        a = ang[th * P:(th + 1) * P]
        t[:, COS + th * 64:COS + th * 64 + 64] = np.cos(a)
        t[:, SIN + th * 64:SIN + th * 64 + 64] = np.sin(a)
    rel = np.arange(256)[None, :] - p[:, None]
    t[:, REL:REL + 256] = np.where(rel >= 0, rel, 1e9)
    t[:, IOTA:IOTA + SEQ] = np.arange(SEQ)
    return t


NAMES = ["x", "norm1_g", "w_in", "q_norm_g", "k_norm_g", "idx_k_ln_w", "idx_k_ln_b", "ret_norm_g", "w_out",
         "norm2_g", "w_group", "w_router", "w1", "w3", "w2"]


def kernel(**inputs):
    import concourse.bacc as bacc
    from concourse.bass_utils import run_bass_kernel_spmd

    nc = bacc.Bacc("TRN2", target_bir_lowering=False, num_devices=1)
    arrays = {f"{name}_dram": np.ascontiguousarray(inputs[name]) for name in NAMES}
    arrays["consts_dram"] = constants()
    args = [nc.dram_tensor(name, a.shape, F32, kind="ExternalInput").ap() for name, a in arrays.items()]
    out = nc.dram_tensor("out_dram", [1, SEQ, D], F32, kind="ExternalOutput").ap()
    build(nc, *args, out)
    r = run_bass_kernel_spmd(nc, [arrays], core_ids=[0])
    return r.results[0]["out_dram"]
```
